# Optimizing a Trainium2 kernel written in Bass

```python
import jax
import jax.numpy as jnp
from jax import lax

D_MODEL = 1024
BATCH = 1
SEQ = 1024
DEPTH = 2
DEC_BATCH = 8
DEC_SEQ = 1
PAST_LEN = 1024
PAGE_SIZE = 128

N_POOL_LAYERS = DEPTH // 2
N_ATTN_LAYERS = DEPTH - N_POOL_LAYERS
POOL_WINDOWS = (2, 4, 8, 16)
POOL_GROUP_W = D_MODEL // len(POOL_WINDOWS)
POOL_HIST = max(POOL_WINDOWS) - 1
D_FF = 2816
CONV_W = 3
ATTN_GROUPS = ((128, 1), (512, 4), (2048, 16))
N_GROUPS = len(ATTN_GROUPS)
HEADS_PER_GROUP = 8
HEAD_DIM = 64
ROT_DIM = HEAD_DIM // 4
ROPE_THETA = 500000.0
ATTN_BLOCK = 128
NORM_EPS = 1e-6
NEG_INF = -1e30

kernel_name = "yoco_pool_dilated_decoder_step"

def rms_norm(x, g):
    xf = x.astype(jnp.float32)
    y = xf * lax.rsqrt(jnp.mean(xf * xf, axis=-1, keepdims=True) + NORM_EPS)
    return (y * g.astype(jnp.float32)).astype(x.dtype)

def rotary(x, pos):
    inv_freq = ROPE_THETA ** (-jnp.arange(0, ROT_DIM, 2, dtype=jnp.float32) / ROT_DIM)
    ang = pos.astype(jnp.float32)[:, None] * inv_freq[None, :]
    shape = (1, pos.shape[0]) + (1,) * (x.ndim - 3) + (ROT_DIM // 2,)
    cos = jnp.cos(ang).reshape(shape)
    sin = jnp.sin(ang).reshape(shape)
    xf = x.astype(jnp.float32)
    x1 = xf[..., : ROT_DIM // 2]
    x2 = xf[..., ROT_DIM // 2: ROT_DIM]
    out = jnp.concatenate([x1 * cos - x2 * sin, x2 * cos + x1 * sin, xf[..., ROT_DIM:]], axis=-1)
    return out.astype(x.dtype)

def pool_mixer(ext, n_hist, pos, w_pool, scale):
    B, L, D = ext.shape
    T = L - n_hist
    ef = ext.astype(jnp.float32)
    csum = jnp.concatenate([jnp.zeros((B, 1, D), jnp.float32), jnp.cumsum(ef, axis=1)], axis=1)
    hi = csum[:, n_hist + 1:]
    cur = ef[:, n_hist:]
    t_end = jnp.arange(T) + n_hist + 1
    parts = []
    for g, w in enumerate(POOL_WINDOWS):
        sl = slice(g * POOL_GROUP_W, (g + 1) * POOL_GROUP_W)
        lo = jnp.take(csum[..., sl], jnp.maximum(t_end - w, 0), axis=1)
        cnt = jnp.minimum(pos + 1, w).astype(jnp.float32)[None, :, None]
        parts.append((hi[..., sl] - lo) / cnt - cur[..., sl])
    d = jnp.stack(parts, axis=2)
    mixed = jnp.einsum('btgc,gce->btge', d, w_pool.astype(jnp.float32)).reshape(B, T, D)
    return (mixed * scale.astype(jnp.float32)).astype(ext.dtype)

def conv_ffn(x, hist, g, w_up, cw, cb, w_down):
    h = rms_norm(x, g)
    u = jnp.einsum('btd,df->btf', h, w_up)
    ext = jnp.concatenate([hist.astype(u.dtype), u], axis=1)
    T = u.shape[1]
    c = cb + sum(cw[j] * ext[:, j: j + T] for j in range(CONV_W))
    a, b = jnp.split(c, 2, axis=-1)
    out = jnp.einsum('btf,fd->btd', jax.nn.silu(a) * b, w_down)
    return out, ext[:, -(CONV_W - 1):]

def shared_kv(x, pos, g_kv, w_kv, k_gain):
    B, T, _ = x.shape
    kv = jnp.einsum('btd,de->bte', rms_norm(x, g_kv), w_kv)
    kv = kv.reshape(B, T, 2, N_GROUPS, HEADS_PER_GROUP, HEAD_DIM)
    k = rotary(rms_norm(kv[:, :, 0], k_gain), pos)
    return k, kv[:, :, 1]

def project_q(x, pos, g, w_q, q_gain):
    B, T, _ = x.shape
    q = jnp.einsum('btd,de->bte', rms_norm(x, g), w_q)
    q = q.reshape(B, T, N_GROUPS, HEADS_PER_GROUP, HEAD_DIM)
    return rotary(rms_norm(q, q_gain), pos) * (HEAD_DIM ** -0.5)

def dilated_prompt(q, k, v, dil, n_back):
    B, S, H, E = q.shape
    L = S // dil
    nb = -(-L // ATTN_BLOCK)
    Lp = nb * ATTN_BLOCK

    def blocks(a):
        a = a.reshape(B, L, dil, H, E)
        a = jnp.pad(a, ((0, 0), (0, Lp - L), (0, 0), (0, 0), (0, 0)))
        return a.reshape(B, nb, ATTN_BLOCK, dil, H, E)

    def with_prev(a):
        prev = jnp.concatenate([jnp.zeros_like(a[:, :1]), a[:, :-1]], axis=1)
        return jnp.concatenate([prev, a], axis=2)

    qb = blocks(q)
    kk = with_prev(blocks(k))
    vv = with_prev(blocks(v))
    s = jnp.einsum('bnqrhe,bnkrhe->bnrhqk', qb, kk).astype(jnp.float32)
    qi = jnp.arange(ATTN_BLOCK)[:, None] + ATTN_BLOCK
    ki = jnp.arange(2 * ATTN_BLOCK)[None, :]
    dist = qi - ki
    key_idx = jnp.arange(nb)[:, None, None] * ATTN_BLOCK - ATTN_BLOCK + ki[None]
    mask = ((dist >= 0) & (dist <= n_back))[None] & (key_idx >= 0)
    s = jnp.where(mask[None, :, None, None], s, NEG_INF)
    lse = jax.nn.logsumexp(s, axis=-1)
    p = jnp.exp(s - lse[..., None])
    o = jnp.einsum('bnrhqk,bnkrhe->bnqrhe', p, vv.astype(jnp.float32))
    o = o.reshape(B, Lp, dil, H, E)[:, :L].reshape(B, S, H, E)
    lse = jnp.transpose(lse, (0, 1, 4, 2, 3)).reshape(B, Lp, dil, H)[:, :L].reshape(B, S, H)
    return o, lse

def dilated_sample(q, k_buf, v_buf, k_new, v_new, dil, n_back):
    n_buf = k_buf.shape[1]
    T = q.shape[1]
    kext = jnp.concatenate([k_buf.astype(k_new.dtype), k_new], axis=1)
    vext = jnp.concatenate([v_buf.astype(v_new.dtype), v_new], axis=1)
    idx = n_buf + jnp.arange(T)[:, None] - dil * jnp.arange(n_back + 1)[None, :]
    valid = idx >= 0
    idx = jnp.maximum(idx, 0)
    kg = jnp.take(kext, idx, axis=1)
    vg = jnp.take(vext, idx, axis=1)
    s = jnp.einsum('bthe,btkhe->bthk', q, kg).astype(jnp.float32)
    s = jnp.where(valid[None, :, None, :], s, NEG_INF)
    lse = jax.nn.logsumexp(s, axis=-1)
    p = jnp.exp(s - lse[..., None])
    o = jnp.einsum('bthk,btkhe->bthe', p, vg.astype(jnp.float32))
    return o, lse

def dilated_mixer(q, k, v, kv_hist, w_o):
    B, T = q.shape[:2]
    outs, lses = [], []
    for g, (win, dil) in enumerate(ATTN_GROUPS):
        n_back = win // dil
        if kv_hist is None:
            o, lse = dilated_prompt(q[:, :, g], k[:, :, g], v[:, :, g], dil, n_back)
        else:
            buf = kv_hist[g]
            o, lse = dilated_sample(q[:, :, g], buf[:, :, 0], buf[:, :, 1], k[:, :, g], v[:, :, g], dil, n_back)
        outs.append(o)
        lses.append(lse)
    wts = jax.nn.softmax(jnp.stack(lses, axis=0), axis=0)
    o = jnp.sum(wts[..., None] * jnp.stack(outs, axis=0), axis=0)
    return jnp.einsum('bte,ed->btd', o.reshape(B, T, HEADS_PER_GROUP * HEAD_DIM).astype(q.dtype), w_o)

def trunk(x, pos, pool_hist, conv_hist, kv_hist, g_pool, w_pool, pool_scale, g_ffn, w_up, conv_w,
          conv_b, w_down, g_kv, w_kv, k_gain, g_attn, w_q, q_gain, w_o):
    B, T, _ = x.shape
    new_pool, new_conv = [], []
    k_sh = v_sh = None
    for layer in range(DEPTH):
        if layer < N_POOL_LAYERS:
            xn = rms_norm(x, g_pool[layer])
            if pool_hist is None:
                ext, n_hist = xn, 0
            else:
                ext = jnp.concatenate([pool_hist[layer].astype(xn.dtype), xn], axis=1)
                n_hist = pool_hist.shape[2]
            x = x + pool_mixer(ext, n_hist, pos, w_pool[layer], pool_scale[layer])
            new_pool.append(ext[:, -POOL_HIST:])
        else:
            if layer == N_POOL_LAYERS:
                k_sh, v_sh = shared_kv(x, pos, g_kv, w_kv, k_gain)
            j = layer - N_POOL_LAYERS
            q = project_q(x, pos, g_attn[j], w_q[j], q_gain[j])
            x = x + dilated_mixer(q, k_sh, v_sh, kv_hist, w_o[j])
        if conv_hist is None:
            hist = jnp.zeros((B, CONV_W - 1, 2 * D_FF), x.dtype)
        else:
            hist = conv_hist[layer]
        f_out, h_new = conv_ffn(x, hist, g_ffn[layer], w_up[layer], conv_w[layer], conv_b[layer], w_down[layer])
        x = x + f_out
        new_conv.append(h_new)
    kv_new = []
    for g, (win, _) in enumerate(ATTN_GROUPS):
        rows = jnp.stack([k_sh[:, :, g], v_sh[:, :, g]], axis=2)
        kv_new.append(rows[:, -min(win, T):] if kv_hist is None else rows)
    return x, jnp.stack(new_pool, axis=0), jnp.stack(new_conv, axis=0), kv_new

def setup_inputs(seed: int = 0) -> dict:
    key = jax.random.key(seed)
    ks = jax.random.split(key, 22)
    f32 = jnp.float32

    def nrm(k, shape, s):
        return jax.random.normal(k, shape, f32) * s

    qkv_w = N_GROUPS * HEADS_PER_GROUP * HEAD_DIM
    out_w = HEADS_PER_GROUP * HEAD_DIM
    kv_shape = lambda win: (DEC_BATCH, min(win, PAST_LEN), 2, HEADS_PER_GROUP, HEAD_DIM)
    return {
        'x_prompt': nrm(ks[0], (BATCH, SEQ, D_MODEL), 1.0),
        'x_sample': nrm(ks[1], (DEC_BATCH, DEC_SEQ, D_MODEL), 1.0),
        'state_pool': nrm(ks[2], (N_POOL_LAYERS, DEC_BATCH, POOL_HIST, D_MODEL), 1.0),
        'state_conv': nrm(ks[3], (DEPTH, DEC_BATCH, CONV_W - 1, 2 * D_FF), 1.0),
        'cache_kv_w128': nrm(ks[4], kv_shape(ATTN_GROUPS[0][0]), 1.0),
        'cache_kv_w512': nrm(ks[5], kv_shape(ATTN_GROUPS[1][0]), 1.0),
        'cache_kv_w2048': nrm(ks[6], kv_shape(ATTN_GROUPS[2][0]), 1.0),
        'g_pool': 1.0 + nrm(ks[7], (N_POOL_LAYERS, D_MODEL), 0.05),
        'w_pool': nrm(ks[8], (N_POOL_LAYERS, len(POOL_WINDOWS), POOL_GROUP_W, POOL_GROUP_W), POOL_GROUP_W ** -0.5),
        'pool_scale': 1.0 + nrm(ks[9], (N_POOL_LAYERS, D_MODEL), 0.05),
        'g_ffn': 1.0 + nrm(ks[10], (DEPTH, D_MODEL), 0.05),
        'w_up': nrm(ks[11], (DEPTH, D_MODEL, 2 * D_FF), D_MODEL ** -0.5),
        'conv_w': nrm(ks[12], (DEPTH, CONV_W, 2 * D_FF), CONV_W ** -0.5),
        'conv_b': nrm(ks[13], (DEPTH, 2 * D_FF), 0.01),
        'w_down': nrm(ks[14], (DEPTH, D_FF, D_MODEL), D_FF ** -0.5),
        'g_kv': 1.0 + nrm(ks[15], (D_MODEL,), 0.05),
        'w_kv': nrm(ks[16], (D_MODEL, 2 * qkv_w), D_MODEL ** -0.5),
        'k_gain': 1.0 + nrm(ks[17], (HEAD_DIM,), 0.05),
        'g_attn': 1.0 + nrm(ks[18], (N_ATTN_LAYERS, D_MODEL), 0.05),
        'w_q': nrm(ks[19], (N_ATTN_LAYERS, D_MODEL, qkv_w), D_MODEL ** -0.5),
        'q_gain': 1.0 + nrm(ks[20], (N_ATTN_LAYERS, HEAD_DIM), 0.05),
        'w_o': nrm(ks[21], (N_ATTN_LAYERS, out_w, D_MODEL), out_w ** -0.5),
    }

def reference(x_prompt, x_sample, state_pool, state_conv, cache_kv_w128, cache_kv_w512, cache_kv_w2048,
              g_pool, w_pool, pool_scale, g_ffn, w_up, conv_w, conv_b, w_down, g_kv, w_kv, k_gain,
              g_attn, w_q, q_gain, w_o):
    pos_p = jnp.arange(x_prompt.shape[1], dtype=jnp.int32)
    y_p, pool_p, conv_p, kv_p = trunk(x_prompt, pos_p, None, None, None, g_pool, w_pool, pool_scale,
                                      g_ffn, w_up, conv_w, conv_b, w_down, g_kv, w_kv, k_gain,
                                      g_attn, w_q, q_gain, w_o)
    pos_s = PAST_LEN + jnp.arange(x_sample.shape[1], dtype=jnp.int32)
    y_s, pool_s, conv_s, kv_s = trunk(x_sample, pos_s, state_pool, state_conv,
                                      (cache_kv_w128, cache_kv_w512, cache_kv_w2048),
                                      g_pool, w_pool, pool_scale, g_ffn, w_up, conv_w, conv_b, w_down,
                                      g_kv, w_kv, k_gain, g_attn, w_q, q_gain, w_o)
    return (y_p, y_s, pool_p, pool_s, conv_p, conv_s, kv_p[0], kv_s[0], kv_p[1], kv_s[1], kv_p[2], kv_s[2])


_drawn_inputs = setup_inputs


def setup_inputs(seed=0):
    import zlib

    import numpy as np

    out = dict(_drawn_inputs(seed))
    spreads = {}
    factors = {'conv_b': 6.611, 'g_attn': 8.0, 'q_gain': 8.0}
    for name, (base, spread) in spreads.items():
        noise = np.random.default_rng([zlib.crc32(name.encode()), seed]).standard_normal(out[name].shape)
        drawn = base * np.exp(spread * noise) if base else spread * noise
        out[name] = jnp.asarray(drawn.astype(out[name].dtype))
    for name, factor in factors.items():
        out[name] = (out[name] * factor).astype(out[name].dtype)
    return out
```

```python
from contextlib import ExitStack

import numpy as np

import concourse.bass as bass
import concourse.mybir as mybir

P = 128
D = 1024
T = 1024
NS = 8
N = T + NS
NC = 3
NW = N // NC
KC = D // P
F = 2816
NF = F // P
NB = NF // 2
LAST = NB - 1
SLABS = 3 * NF
DEPTH = 2
HIST = 15
TAIL = HIST + NS
CT = 2 + NS
PAD = 16
WINDOWS = (2, 4, 8, 16)
GROUPS = 3
HEADS = 8
HD = 64
QW = HEADS * HD
DIL = (1, 4, 16)
HW = QW // 2
OW = QW + 2 * HEADS
SK = 129 + 129 + 65
NV = 5
EPS = 1e-6
NEG = -1e30

F32 = mybir.dt.float32
F32R = mybir.dt.float32r
BF16 = mybir.dt.bfloat16
ALU = mybir.AluOpType
ACT = mybir.ActivationFunctionType
AX = mybir.AxisListType

G_POOL, G_SCALE, G_FFN, G_KV, G_ATTN = 0, KC, 2 * KC, 4 * KC, 5 * KC


def build(nc, a, o):
    with ExitStack() as ctx:
        def sem(name):
            return ctx.enter_context(nc.semaphore(name))

        def sb(name, shape, dt=F32, scope=ctx):
            return scope.enter_context(nc.sbuf_tensor(name, shape, dt))

        ps = ctx.enter_context(nc.psum_tensor("ps", [P, 8, 512], F32))

        x = sb("x", [P, KC, N])
        convh = sb("convh", [P, NF * 2, 32])
        rb = sb("rb", [P, N])
        acc = sb("acc", [P, N])
        sq = sb("sq", [P, 2, PAD + N])
        ident = sb("ident", [P, P])
        ones = sb("ones", [P, P])
        cwT = sb("cwT", [P, DEPTH * 3 * 2 * NF])
        cbT = sb("cbT", [P, DEPTH * 2 * NF])
        gT = sb("gT", [P, 6 * KC])
        sel = sb("sel", [NS * HIST, 4, NS])
        invc = sb("invc", [P, 4, PAD])
        hsum = sb("hsum", [P, KC, NS])
        utail = sb("utail", [P, 2 * NF, CT])
        ctm = sb("ctm", [CT, 2, 512])
        rtok = sb("rtok", [P, 9])
        rtmp = sb("rtmp", [P, 4, 9])
        stage = sb("stage", [P, 3, 1024])

        r1 = ExitStack()
        xh = sb("xh", [P, KC, N], F32R, r1)
        xl = sb("xl", [P, KC, N], F32R, r1)
        r1.close()
        r1 = ExitStack()
        xin = sb("xin", [P, 8, D], F32, r1)
        xsin = sb("xsin", [NS, D], F32, r1)
        phist = sb("phist", [NS * HIST, D], F32, r1)
        chin = sb("chin", [32, 2 * F], F32, r1)
        vA = sb("vA", [88, 3, P], F32, r1)
        vB = sb("vB", [88, P], F32, r1)
        vC = sb("vC", [48, P], F32, r1)
        r1.close()
        r1 = ExitStack()
        qt = sb("qt", [P, 2, QW], F32, r1)
        kvt = sb("kvt", [P, 4, 2 * QW], F32, r1)
        qT = sb("qT", [P, 2, QW], F32, r1)
        kT = sb("kT", [P, 3, QW], F32, r1)
        prob = sb("prob", [P, 2, 1024], F32, r1)
        probT = sb("probT", [P, 2, 1024], F32, r1)
        osb = sb("osb", [P, 3, OW], F32, r1)
        maskf = sb("maskf", [P, 3, P], F32, r1)
        mask = sb("mask", [P, 3, QW], BF16, r1)
        identb = sb("identb", [P, P], BF16, r1)
        qn = sb("qn", [NS, GROUPS, QW], F32, r1)
        samp = sb("samp", [P, 84], F32, r1)
        r1.close()
        r1 = ExitStack()
        om = sb("om", [P, 2, GROUPS, OW], F32, r1)
        ow = sb("ow", [P, 2, 4, GROUPS * HEADS], F32, r1)
        ot = sb("ot", [P, 2, 2, QW], F32, r1)
        yst = sb("yst", [P, 2, 8, P], F32, r1)
        yss = sb("yss", [NS, D], F32, r1)
        r1.close()
        sb("region1", [P, 2 * KC, N], F32, ctx)

        r2 = ExitStack()
        wh = sb("wh", [P, 3, 1024], F32R, r2)
        wl = sb("wl", [P, 3, 1024], F32R, r2)
        ua = sb("ua", [P, 2 + N], F32, r2)
        ub = sb("ub", [P, 2 + N], F32, r2)
        ca = sb("ca", [P, N], F32, r2)
        cb = sb("cb", [P, N], F32, r2)
        gh = sb("gh", [P, 2, N], F32R, r2)
        gl = sb("gl", [P, 2, N], F32R, r2)
        r2.close()
        r2 = ExitStack()
        sb("over_w", [P, 6, 1024], F32, r2)
        xn = sb("xn", [P, KC, PAD + N], F32, r2)
        swin = sb("swin", [P, 2, PAD + N], F32, r2)
        r2.close()

        r2 = ExitStack()
        wp1h = sb("wp1h", [P, KC, HW], F32R, r2)
        wp1l = sb("wp1l", [P, KC, HW], F32R, r2)
        sb("over_w1", [P, 2048], F32, r2)
        wp0h = sb("wp0h", [P, KC, HW], F32R, r2)
        wp0l = sb("wp0l", [P, KC, HW], F32R, r2)
        sb("over_u", [P, 36], F32, r2)
        wp2h = sb("wp2h", [P, KC, HW], F32R, r2)
        wp2l = sb("wp2l", [P, KC, HW], F32R, r2)
        sb("over_g", [P, 32], F32, r2)
        kn = sb("kn", [P, 3, QW], F32, r2)
        rot = sb("rot", [P, 2, 9, 16], F32, r2)
        hg = sb("hg", [P, 2, HD], F32, r2)
        hs = sb("hs", [P, 5, HEADS], F32, r2)
        r2.close()
        wph, wpl = (wp0h, wp1h, wp2h), (wp0l, wp1l, wp2l)
        r2 = ExitStack()
        oTh = sb("oTh", [P, 4, N], F32R, r2)
        oTl = sb("oTl", [P, 4, N], F32R, r2)
        r2b = ExitStack()
        qb = sb("qb", [P, 2, GROUPS, QW], F32, r2b)
        kc = sb("kc", [P, 3, QW], F32, r2b)
        vc = sb("vc", [P, NV, QW], F32, r2b)
        prod = sb("prod", [P, 1, QW], F32, r2b)
        r2b.close()
        woh = sb("woh", [P, 4, D], F32R, r2)
        wol = sb("wol", [P, 4, D], F32R, r2)
        r2.close()
        sq_flat = sq[:, :, :].rearrange("p s n -> p (s n)")
        sc = sq_flat[:, 0:192]
        sall = sq_flat[0:64, 192:192 + SK]
        pT = sq_flat[:, 520:520 + 3 * NS * 32]
        snew = sq_flat[0:NS, 1288:1312]
        bnew = sq_flat[0:NS, 1312:1504]
        stat = sq_flat[0:64, 1504:1508]
        an = sq_flat[0:64, 1508:1532]
        pnew = sq_flat[0:NS, 1532:1556]
        selS = samp[:, 0:4]
        sel8 = samp[0:64, 4:12]
        del8 = samp[0:64, 12:20]
        del64 = samp[0:NS, 20:84]
        diag = kc[:, 0, :]
        om1 = rb[:, 0:QW]
        om2 = acc[:, 0:QW]
        onew = rb[0:NS, QW:2 * QW]

        kvs = nc.dram_tensor("kvs", [GROUPS, N, 2, QW], F32, kind="Internal").ap()
        qs = nc.dram_tensor("qs", [GROUPS, N, QW], F32, kind="Internal").ap()
        os_ = nc.dram_tensor("os_", [GROUPS, T, OW], F32, kind="Internal").ap()

        in_id, in_ph, in_xs, in_v, in_ch = (sem(n) for n in ("in_id", "in_ph", "in_xs", "in_v", "in_ch"))
        in_x = [sem(f"in_x{i}") for i in range(4)]
        set0 = sem("set0")
        pro_pe = sem("pro_pe")
        pro_v = sem("pro_v")
        pro_a = sem("pro_a")
        vec = sem("vec")
        ssq = sem("ssq")
        rn = sem("rn")
        rn_a = sem("rn_a")
        dg = sem("dg")
        rb_pe = sem("rb_pe")
        rb_v = sem("rb_v")
        wp_in, wp_h, wp_l = sem("wp_in"), sem("wp_h"), sem("wp_l")
        xn_v = sem("xn_v")
        tl_pe, tl_a = sem("tl_pe"), sem("tl_a")
        win_v, win_p = sem("win_v"), sem("win_p")
        dif = sem("dif")
        dif_h, dif_l = sem("dif_h"), sem("dif_l")
        pool_pe, pool_x = sem("pool_pe"), sem("pool_x")
        out_w = sem("out_w")
        tl_out = sem("tl_out")

        split_sq, split_acc = sem("split_sq"), sem("split_acc")
        split_hi, split_lo = sem("split_hi"), sem("split_lo")

        class Split:
            def __init__(self, n):
                self.sq = self.hi = self.lo = KC * n
                self.acc = (KC - 1) * n

        ffn_stage = [sem(f"ffn_stage{i}") for i in range(3)]
        ct_out = [sem(f"ct_out{i}") for i in range(2)]

        class Ffn:
            def __init__(self, L):
                n = f"f{L}_"
                self.stage = 16 * SLABS // 3 * L
                self.ct_out = [32 * 6 * L, 32 * 5 * L]
                self.hi = sem(n + "hi")
                self.lo = sem(n + "lo")
                self.up = sem(n + "up")
                self.down = sem(n + "down")
                self.A = sem(n + "A")
                self.B = sem(n + "B")
                self.norm = sem(n + "norm")
                self.r = sem(n + "r")
                self.ra = sem(n + "ra")
                self.ut = sem(n + "ut")
                self.tap = sem(n + "tap")
                self.conv = sem(n + "conv")
                self.silu = sem(n + "silu")
                self.prod = sem(n + "prod")
                self.gh = sem(n + "gh")
                self.gl = sem(n + "gl")
                self.ct_pe = sem(n + "ct_pe")
                self.ct = sem(n + "ct")

        split = [Split(0), Split(1), Split(2)]
        ffn = [Ffn(0), Ffn(1)]
        in_rot = sem("in_rot")
        piece_in = [sem(f"piece_in{i}") for i in range(3)]
        pj_h, pj_l = sem("pj_h"), sem("pj_l")
        pj_pe = sem("pj_pe")
        pj_a = sem("pj_a")
        pj_sq, pj_rt = sem("pj_sq"), sem("pj_rt")
        pj_s = sem("pj_s")
        pj_v = sem("pj_v")
        pj_r = sem("pj_r")
        rows_out = [sem(f"rows_out{i}") for i in range(3)]
        kv_out = sem("kv_out")
        at_q = [sem(f"at_q{i}") for i in range(2)]
        at_kv = [sem(f"at_kv{i}") for i in range(4)]
        at_tp, at_tc = sem("at_tp"), sem("at_tc")
        at_mk = sem("at_mk")
        at_s = sem("at_s")
        at_m = sem("at_m")
        at_e = sem("at_e")
        at_pt = sem("at_pt")
        at_pa, at_pb = sem("at_pa"), sem("at_pb")
        at_o, at_oc = sem("at_o"), sem("at_oc")
        in_new, in_diag = sem("in_new"), sem("in_diag")
        sm_q = [sem(f"sm_q{i}") for i in range(2)]
        sm_k = [sem(f"sm_k{i}") for i in range(3)]
        sm_vin = [sem(f"sm_vin{i}") for i in range(NV)]
        sm_z = sem("sm_z")
        sm_p, sm_r = sem("sm_p"), sem("sm_r")
        sm_new = sem("sm_new")
        sm_pe = sem("sm_pe")
        sm_e = sem("sm_e")
        sm_st = sem("sm_st")
        sm_o = sem("sm_o")
        sm_f, sm_fh, sm_fl = sem("sm_f"), sem("sm_fh"), sem("sm_fl")
        mg_in = [sem(f"mg_in{i}") for i in range(2)]
        mg_a, mg_e, mg_v, mg_p = sem("mg_a"), sem("mg_e"), sem("mg_v"), sem("mg_p")
        mg_pe, mg_h, mg_l = sem("mg_pe"), sem("mg_h"), sem("mg_l")
        wo_h, wo_l, wo_pe, wo_x = sem("wo_h"), sem("wo_l"), sem("wo_pe"), sem("wo_x")
        y_pe, y_a, y_v, y_s, ys_out = sem("y_pe"), sem("y_a"), sem("y_v"), sem("y_s"), sem("ys_out")
        block = ctx.enter_context(nc.Block())

        def wait(e, s, v):
            if not isinstance(v, int) or v > 0:
                e.wait_ge(s, v)

        def bank3(s):
            return ps[:, 3 * s:3 * s + 3, 0:NW]

        def cols3(t):
            return t.rearrange("p (c n) -> p c n", c=NC)

        def group(pe, bank0, parts, pre=None):
            for i, (w, m) in enumerate(parts):
                if pre:
                    pre(i)
                for c in range(NC):
                    mm = pe.matmul(ps[:, bank0 + c, 0:NW], w, m[:, c * NW:(c + 1) * NW],
                                   start=(i == 0), stop=(i == len(parts) - 1))
            return mm

        def three(w_hi, w_lo, m_hi, m_lo):
            return [(w_hi, m_hi), (w_hi, m_lo), (w_lo, m_hi)]

        def act_split(act, S, d, gain):
            if d >= 3:
                act.wait_ge(split_acc, S.acc + d - 2)
            nc.scalar.activation(acc[:, :] if d == 0 else sq[:, d % 2, 0:N], x[:, d, :], ACT.Square).then_inc(split_sq, 1)
            if gain is None:
                nc.scalar.activation(xh[:, d, :], x[:, d, :], ACT.Copy).then_inc(split_hi, 1)
            else:
                nc.scalar.activation(xh[:, d, :], x[:, d, :], ACT.Copy,
                                     scale=gT[:, gain + d:gain + d + 1]).then_inc(split_hi, 1)

        def dve_split(v, S, d, gain):
            v.wait_ge(split_hi, S.hi + d + 1)
            if gain is None:
                nc.vector.tensor_tensor(xl[:, d, :], x[:, d, :], xh[:, d, :].bitcast(F32), ALU.subtract).then_inc(split_lo, 1)
            else:
                nc.vector.scalar_tensor_tensor(out=xl[:, d, :], in0=x[:, d, :], scalar=gT[:, gain + d:gain + d + 1],
                                               in1=xh[:, d, :].bitcast(F32), op0=ALU.mult,
                                               op1=ALU.subtract).then_inc(split_lo, 1)

        def pool_split(g, S):
            for d in range(1, KC):
                g.wait_ge(split_sq, S.sq + d + 1)
                if d >= 2:
                    g.wait_ge(split_acc, S.acc + d - 1)
                nc.gpsimd.tensor_tensor(acc[:, :], acc[:, :], sq[:, d % 2, 0:N], ALU.add).then_inc(split_acc, 1)

        CH = 16

        def sp_start(sp):
            sp.dma_start(ident[:, :], a["ident"]).then_inc(in_id, 16)
            for i in range(4):
                sp.dma_start(xin[:, 2 * i:2 * i + 2, :], a["x_prompt"][0, 2 * i * P:(2 * i + 2) * P, :].rearrange(
                    "(t p) d -> p t d", p=P)).then_inc(in_x[i], 16)
            sp.dma_start(xsin[:, :], a["x_sample"].rearrange("s o d -> (s o) d")).then_inc(in_xs, 16)
            for g0, n, src in ((G_POOL, KC, a["g_pool"]), (G_SCALE, KC, a["pool_scale"]), (G_FFN, 2 * KC, a["g_ffn"]),
                               (G_ATTN, KC, a["g_attn"])):
                sp.dma_start(vC[g0:g0 + n, :], src.rearrange("l (c p) -> (l c) p", p=P)).then_inc(in_v, 16)
            sp.dma_start(vC[G_KV:G_KV + KC, :], a["g_kv"].rearrange("(c p) -> c p", p=P)).then_inc(in_v, 16)
            sp.dma_start(vB[:, :], a["conv_b"].rearrange("l (c p) -> (l c) p", p=P)).then_inc(in_v, 16)
            sp.dma_start(vA[:, :, :], a["conv_w"].rearrange("l j (c p) -> (l j c) p", p=P).rearrange(
                "(b q) p -> q b p", q=88)).then_inc(in_v, 16)
            sp.dma_start(sel[:, :, :], a["sel"]).then_inc(in_ph, 16)
            sp.dma_start(invc[:, :, :], a["invc"]).then_inc(in_ph, 16)
            sp.dma_start(phist[:, :], a["state_pool"][0].rearrange("s h d -> (s h) d")).then_inc(in_ph, 16)
            sp.dma_start(stage[:, 1:3, :].rearrange("p s n -> p (s n)").rearrange("p (q e) -> p q e", e=256),
                         a["w_pool"][0].rearrange("g (k p) e -> p (g k) e", p=P)).then_inc(wp_in, 16)
            sp.dma_start(chin[:, :], a["state_conv"].rearrange("l s j f -> (l s j) f")).then_inc(in_ch, 16)
            sp.dma_start(o["pool_sample"][0, :, 0:HIST - 1, :], a["state_pool"][0, :, 1:HIST, :]).then_inc(out_w, 16)
            for L in range(DEPTH):
                sp.dma_start(o["conv_sample"][L, :, 0, :], a["state_conv"][L, :, 1, :]).then_inc(out_w, 16)

        def sp_pool_tails(sp):
            sp.wait_ge(tl_a, 2)
            sp.dma_start(o["pool_prompt"][0, 0], acc[0:HIST, 0:D]).then_inc(tl_out, 16)
            sp.dma_start(o["pool_sample"][0, :, HIST - 1, :], acc[HIST:TAIL, 0:D]).then_inc(tl_out, 16)

        def pe_start(pe):
            pe.wait_ge(in_id, 16)
            for g in range(22):
                b = g % 8
                if g >= 8:
                    pe.wait_ge(pro_v if g % 2 == 0 else pro_a, (g - 8) // 2 + 1)
                if g < 16:
                    pe.wait_ge(in_x[g // 4], 16)
                    for i in range(4):
                        d = 4 * (g % 2) + i
                        mm = pe.transpose(ps[:, b, i * P:(i + 1) * P], xin[:, g // 2, d * P:(d + 1) * P], ident[:, :])
                elif g == 16:
                    pe.wait_ge(in_xs, 16)
                    for d in range(KC):
                        mm = pe.transpose(ps[:, b, d * NS:(d + 1) * NS], xsin[:, d * P:(d + 1) * P], ident[0:NS, 0:NS])
                elif g == 17:
                    pe.wait_ge(in_v, 16 * 7)
                    pe.transpose(ps[:, b, 0:48], vC[:, :], ident[0:48, 0:48])
                    pe.transpose(ps[:, b, 48:136], vB[:, :], ident[0:88, 0:88])
                    for i in range(3):
                        mm = pe.transpose(ps[:, b, 136 + 88 * i:224 + 88 * i], vA[:, i, :], ident[0:88, 0:88])
                elif g == 18:
                    pe.wait_ge(in_ph, 16 * 3)
                    for d in range(KC):
                        mm = pe.matmul(ps[:, b, d * NS:(d + 1) * NS], phist[:, d * P:(d + 1) * P], sel[:, d // 2, :],
                                       start=True, stop=True)
                else:
                    if g == 19:
                        pe.wait_ge(pro_v, 8)
                        pe.wait_ge(pro_a, 8)
                        pe.wait_ge(dg, 9)
                        pe.wait_ge(set0, 2)
                        for c in range(NC):
                            mm = pe.matmul(ps[:, 5 + c, 0:NW], ones[:, :], acc[:, c * NW:(c + 1) * NW],
                                           start=True, stop=True)
                        mm.then_inc(rb_pe, 1)
                        pe.wait_ge(in_ch, 16)
                    if g == 21:
                        pe.wait_ge(rb_v, 1)
                    for i in range(CH * (g - 19), min(CH * (g - 18), 2 * NF)):
                        c = i - CH * (g - 19)
                        mm = pe.transpose(ps[:, b, 32 * c:32 * c + 32], chin[:, i * P:(i + 1) * P], ident[0:32, 0:32])
                mm.then_inc(pro_pe, 1)

        def pro_copy(g):
            b = g % 8
            if g < 16:
                return [(x[:, 4 * (g % 2):4 * (g % 2) + 4, (g // 2) * P:(g // 2 + 1) * P],
                         ps[:, b, :].rearrange("p (i n) -> p i n", i=4))]
            if g == 16:
                return [(x[:, :, T:N], ps[:, b, 0:KC * NS].rearrange("p (i n) -> p i n", i=KC))]
            if g == 17:
                return [(gT[:, :], ps[:, b, 0:48]), (cbT[:, :], ps[:, b, 48:136]), (cwT[:, :], ps[:, b, 136:400])]
            if g == 18:
                return [(hsum[:, :, :], ps[:, b, 0:KC * NS].rearrange("p (i n) -> p i n", i=KC))]
            i0, i1 = CH * (g - 19), min(CH * (g - 18), 2 * NF)
            return [(convh[:, i0:i1, :], ps[:, b, 0:32 * (i1 - i0)].rearrange("p (i n) -> p i n", n=32))]

        def newton(v, m, y, t, s, n, s_a, n_a):
            v.wait_ge(s_a, n_a)
            nc.vector.reciprocal(y, y).then_inc(s, 1)
            v.wait_ge(s, n + 1)
            nc.vector.tensor_tensor(t, y, y, ALU.mult).then_inc(s, 1)
            v.wait_ge(s, n + 2)
            nc.vector.scalar_tensor_tensor(out=t, in0=t, scalar=-0.5, in1=m, op0=ALU.mult, op1=ALU.mult).then_inc(s, 1)
            v.wait_ge(s, n + 3)
            nc.vector.scalar_tensor_tensor(out=y, in0=t, scalar=1.5, in1=y, op0=ALU.add, op1=ALU.mult).then_inc(s, 1)
            v.wait_ge(s, n + 4)

        def dve_windows(v, c, buf, s, n, add):
            cur = xn[:, c, :]
            k, i = 1, 0
            first = (n % 2)
            while k < WINDOWS[c // 2]:
                dst = buf[:, (first + i) % 2, :]
                if i:
                    v.wait_ge(s, n + i)
                lo = 2 * k - 1
                add(dst[:, lo:PAD + T], cur[:, lo:PAD + T], cur[:, lo - k:PAD + T - k]).then_inc(s, 1)
                cur, k, i = dst, 2 * k, i + 1
            return cur, n + i

        def window_plan(par):
            plan, n = {}, 0
            for g in range(4):
                steps = g + 1
                plan[2 * g + par] = (n, (n + steps - 1) % 2, n + steps)
                n += steps
            return plan
        PLAN = {**window_plan(0), **window_plan(1)}

        def dve_start(v):
            for g in range(0, 16, 2):
                v.wait_ge(pro_pe, g + 1)
                for dst, src in pro_copy(g):
                    nc.vector.tensor_copy(dst, src).then_inc(pro_v, 1)
            v.wait_ge(pro_pe, 17)
            for dst, src in pro_copy(16):
                nc.vector.tensor_copy(dst, src).then_inc(pro_v, 1)
            m, y, t = rtmp[:, 0, :], rtok[:, :], rtmp[:, 2, :]
            v.wait_ge(ssq, 9)
            nc.vector.tensor_scalar(m, rtmp[:, 3, :], 1.0 / D, EPS, ALU.mult, ALU.add).then_inc(rn, 1)
            newton(v, m, y, t, rn, 1, rn_a, 1)
            v.wait_ge(in_id, 16)
            for i in range(8):
                nc.vector.tensor_scalar(acc[:, i * P:(i + 1) * P], ident[:, :], rtok[:, i:i + 1], None,
                                        ALU.mult).then_inc(dg, 1)
            nc.vector.tensor_scalar(acc[:, T:N], ident[:, 0:NS], rtok[:, 8:9], None, ALU.mult).then_inc(dg, 1)
            v.wait_ge(pro_pe, 19)
            for dst, src in pro_copy(18):
                nc.vector.tensor_copy(dst, src).then_inc(pro_v, 1)
            v.wait_ge(rb_pe, 1)
            nc.vector.tensor_copy(cols3(rb[:, :]), ps[:, 5:8, 0:NW]).then_inc(rb_v, 1)
            v.wait_ge(rb_v, 1)
            v.wait_ge(vec, 3)
            v.wait_ge(pro_a, 8)
            v.wait_ge(pro_v, 9)
            for c in range(KC):
                nc.vector.scalar_tensor_tensor(out=xn[:, c, PAD:], in0=x[:, c, :], scalar=gT[:, G_POOL + c:G_POOL + c + 1],
                                               in1=rb[:, :], op0=ALU.mult, op1=ALU.mult).then_inc(xn_v, 1)
            v.wait_ge(pro_pe, 21)
            for dst, src in pro_copy(20):
                nc.vector.tensor_copy(dst, src).then_inc(pro_v, 1)
            v.wait_ge(set0, 2)
            v.wait_ge(xn_v, KC)
            v.wait_ge(wp_h, 1)
            nc.vector.tensor_tensor(wl[:, 1:3, :], stage[:, 1:3, :], wh[:, 1:3, :].bitcast(F32), ALU.subtract).then_inc(wp_l, 1)
            dve_ffn_slab0(v, ffn[0])

            def difference(c, i):
                w, par = WINDOWS[c // 2], c % 2
                n, last, done = PLAN[c]
                s = (sq if par else swin)[:, last, :]
                v.wait_ge(win_p if par else win_v, done)
                nc.vector.tensor_tensor(s[:, PAD:2 * PAD], s[:, PAD:2 * PAD], invc[:, c // 2, :], ALU.mult).then_inc(dif, 1)
                nc.vector.tensor_tensor(s[:, PAD + T:], hsum[:, c, :], xn[:, c, PAD + T:], ALU.add).then_inc(dif, 1)
                nc.vector.scalar_tensor_tensor(out=s[:, 2 * PAD:PAD + T], in0=s[:, 2 * PAD:PAD + T], scalar=1.0 / w,
                                               in1=xn[:, c, 2 * PAD:PAD + T], op0=ALU.mult,
                                               op1=ALU.subtract).then_inc(dif, 1)
                v.wait_ge(dif, 5 * i + 1)
                nc.vector.tensor_tensor(s[:, PAD:2 * PAD], s[:, PAD:2 * PAD], xn[:, c, PAD:2 * PAD],
                                        ALU.subtract).then_inc(dif, 1)
                v.wait_ge(dif, 5 * i + 2)
                nc.vector.scalar_tensor_tensor(out=s[:, PAD + T:], in0=s[:, PAD + T:], scalar=1.0 / w,
                                               in1=xn[:, c, PAD + T:], op0=ALU.mult, op1=ALU.subtract).then_inc(dif, 1)

            def tail(c, i):
                last = PLAN[c][1]
                v.wait_ge(dif_h, i + 1)
                nc.vector.tensor_tensor(xl[:, c, :], (sq if c % 2 else swin)[:, last, PAD:], xh[:, c, :].bitcast(F32),
                                        ALU.subtract).then_inc(dif_l, 1)

            v.wait_ge(pro_v, 11)
            for g in range(4):
                if g:
                    v.wait_ge(dif_l, 2 * g)
                    v.wait_ge(dif_h, 2 * g)
                dve_windows(v, 2 * g, swin, win_v, PLAN[2 * g][0],
                            lambda d, p, q: nc.vector.tensor_tensor(d, p, q, ALU.add))
                difference(2 * g, 2 * g)
                difference(2 * g + 1, 2 * g + 1)
                tail(2 * g, 2 * g)
                tail(2 * g + 1, 2 * g + 1)
            for d in range(KC):
                v.wait_ge(pool_pe, d + 1)
                nc.vector.scalar_tensor_tensor(out=cols3(x[:, d, :]), in0=bank3(d % 2), scalar=gT[:, G_SCALE + d:G_SCALE + d + 1],
                                               in1=cols3(x[:, d, :]), op0=ALU.mult, op1=ALU.add).then_inc(pool_x, 1)
                if d % 2 == 1:
                    dve_split(v, split[0], d - 1, G_FFN)
                    dve_split(v, split[0], d, G_FFN)

        def pool_start(g):
            nc.gpsimd.memset(xn[:, :, 0:PAD], 0.0).then_inc(set0, 1)
            nc.gpsimd.memset(ones[:, :], 1.0).then_inc(set0, 1)
            nc.gpsimd.memset(rtmp[:, 3, :], 1.0).then_inc(set0, 1)
            g.wait_ge(xn_v, KC)
            for i in range(4):
                if i:
                    g.wait_ge(dif_l, 2 * i)
                dve_windows(g, 2 * i + 1, sq, win_p, PLAN[2 * i + 1][0],
                            lambda d, p, q: nc.gpsimd.tensor_tensor(d, p, q, ALU.add))
            pool_split(g, split[0])

        def act_start(act):
            act.wait_ge(set0, 3)
            for t in range(8):
                act.wait_ge(in_x[t // 2], 16)
                wait(act, ssq, t)
                nc.scalar.activation(sq[:, 0, 0:D], xin[:, t, :], ACT.Square, accum_out=rtmp[:, 3, t:t + 1]).then_inc(ssq, 1)
                act.wait_ge(pro_pe, 2 * t + 2)
                for dst, src in pro_copy(2 * t + 1):
                    nc.scalar.activation(dst, src, ACT.Copy).then_inc(pro_a, 1)
            act.wait_ge(in_xs, 16)
            act.wait_ge(ssq, 8)
            nc.scalar.activation(sq[0:NS, 0, 0:D], xsin[:, :], ACT.Square, accum_out=rtmp[0:NS, 3, 8:9]).then_inc(ssq, 1)
            act.wait_ge(rn, 1)
            nc.scalar.activation(rtok[:, :], rtmp[:, 0, :], ACT.Sqrt).then_inc(rn_a, 1)
            act.wait_ge(pro_pe, 18)
            for dst, src in pro_copy(17):
                nc.scalar.activation(dst, src, ACT.Copy).then_inc(vec, 1)
            act.wait_ge(wp_in, 16)
            nc.scalar.activation(wh[:, 1:3, :], stage[:, 1:3, :], ACT.Copy).then_inc(wp_h, 1)
            act_ffn_slab0(act, ffn[0], [])
            for g in (19, 21):
                act.wait_ge(pro_pe, g + 1)
                for dst, src in pro_copy(g):
                    nc.scalar.activation(dst, src, ACT.Copy).then_inc(pro_a, 1)
            for h in range(2):
                act.wait_ge(tl_pe, h + 1)
                nc.scalar.activation(acc[0:TAIL, h * 512:(h + 1) * 512], ps[0:TAIL, 6 + h, :], ACT.Copy).then_inc(tl_a, 1)
            for c in range(KC):
                act.wait_ge(dif, 5 * c + 5)
                nc.scalar.activation(xh[:, c, :], (sq if c % 2 else swin)[:, PLAN[c][1], PAD:], ACT.Copy).then_inc(dif_h, 1)
            act.wait_ge(tl_out, 32)
            act.wait_ge(dif_l, KC)
            for d in range(KC):
                act.wait_ge(pool_x, d + 1)
                act.wait_ge(pool_pe, 2 * (d // 2) + 2)
                act_split(act, split[0], d, G_FFN)

        def pe_pool(pe):
            pe.wait_ge(xn_v, KC)
            pe.wait_ge(rb_v, 1)
            for h in range(2):
                for i in range(4):
                    mm = pe.transpose(ps[0:TAIL, 6 + h, i * P:(i + 1) * P], xn[:, 4 * h + i, PAD + N - TAIL:], ident[:, :])
                mm.then_inc(tl_pe, 1)
            pe.wait_ge(wp_l, 1)
            pe.wait_ge(pro_v, 11)
            pe.wait_ge(pro_a, 10)
            pw, pwt = (t[:, 1:3, :].rearrange("p s n -> p (s n)") for t in (wh, wl))
            for g in range(4):
                pe.wait_ge(dif_l, 2 * g + 2)
                for e in range(2):
                    if g:
                        pe.wait_ge(pool_x, 2 * g + e - 1)
                    parts = []
                    for k in range(2):
                        at = (2 * g + k) * 256 + e * P
                        parts += three(pw[:, at:at + P], pwt[:, at:at + P], xh[:, 2 * g + k, :], xl[:, 2 * g + k, :])
                    group(pe, 3 * e, parts).then_inc(pool_pe, 1)


        def slot_of(k):
            return (2 + k) % 3

        def up_src(L, half, f):
            w = a["w_up"][L].rearrange("(k p) n -> p k n", p=P)
            return w[:, :, bass.ds(f * P + half * F, P)]

        def down_src(L, f):
            return a["w_down"][L][bass.ds(f * P, P), :]

        def sp_ffn(sp, L, S, begin):
            def load(n, slot, src, up):
                if isinstance(n, int) and n < 3:
                    begin(sp, n)
                else:
                    sp.wait_ge(S.hi, n - 2)
                    sp.wait_ge(S.lo, n - 2)
                dst = stage[:, slot, :]
                if up:
                    dst = dst.rearrange("p (k n) -> p k n", k=KC)
                sp.dma_start(dst, src).then_inc(ffn_stage[slot], 16)

            load(0, 0, up_src(L, 0, 0), True)
            load(1, 1, up_src(L, 1, 0), True)
            load(2, 2, up_src(L, 0, 1), True)

            def rest(j, last):
                n0 = 6 * j + 2
                load(n0 + 1, slot_of(1), up_src(L, 1, 2 * j + 1), True)
                if last:
                    load(n0 + 2, slot_of(2), down_src(L, 2 * j), False)
                    load(n0 + 3, slot_of(3), down_src(L, 2 * j + 1), False)
                    return
                load(n0 + 2, slot_of(2), up_src(L, 0, 2 * j + 2), True)
                load(n0 + 3, slot_of(3), up_src(L, 1, 2 * j + 2), True)
                load(n0 + 4, slot_of(4), down_src(L, 2 * j), False)
                load(n0 + 5, slot_of(5), down_src(L, 2 * j + 1), False)
                load(n0 + 6, slot_of(6), up_src(L, 0, 2 * j + 3), True)

            with sp.Fori(0, LAST) as j:
                rest(j, False)
            rest(LAST, True)

        def act_slab(act, S, j, k, free):
            act.wait_ge(ffn_stage[slot_of(k)], 32 * j + (S.stage + 16 * ((2 + k) // 3 + 1)))
            for s, v in free:
                wait(act, s, v)
            nc.scalar.activation(wh[:, slot_of(k), :], stage[:, slot_of(k), :], ACT.Copy).then_inc(S.hi, 1)

        def dve_slab(v, S, j, k):
            v.wait_ge(S.hi, 6 * j + 3 + k)
            nc.vector.tensor_tensor(wl[:, slot_of(k), :], stage[:, slot_of(k), :], wh[:, slot_of(k), :].bitcast(F32),
                                    ALU.subtract).then_inc(S.lo, 1)

        def pe_up(pe, S, slot, slab, sset, free, Sx=None):
            pe.wait_ge(S.lo, slab + 1)
            if free is not None:
                pe.wait_ge(*free)
            parts = []
            for k in range(KC):
                w, wt = wh[:, slot, k * P:(k + 1) * P], wl[:, slot, k * P:(k + 1) * P]
                parts += three(w, wt, xh[:, k, :], xl[:, k, :])

            def pre(i):
                if Sx is not None and i % 3 == 0:
                    pe.wait_ge(split_lo, Sx.lo + i // 3 + 1)
            group(pe, 3 * sset, parts, pre).then_inc(S.up, 1)

        def pe_down(pe, S, j, slots, slabs, baseA, baseB, after=None):
            pe.wait_ge(S.lo, slabs)
            pe.wait_ge(S.gl, 2 * j + 2)
            for d in range(KC):
                pe.wait_ge(*((S.A, baseA + d // 2) if d % 2 == 0 else (S.B, baseB + d // 2)))
                parts = []
                for c in range(2):
                    w = wh[:, slots[c], d * P:(d + 1) * P]
                    wt = wl[:, slots[c], d * P:(d + 1) * P]
                    parts += three(w, wt, gh[:, c, :], gl[:, c, :])
                group(pe, 3 * (d % 2), parts).then_inc(S.down, 1)
                if after is not None:
                    after(d)

        def pe_ffn(pe, L, S, Sx, freeA, after=None):
            pe_up(pe, S, 0, 0, 0, freeA, Sx)
            pe.wait_ge(split_acc, Sx.acc + KC - 1)
            for c in range(NC):
                mm = pe.matmul(ps[:, 3 + c, 0:NW], ones[:, :], acc[:, c * NW:(c + 1) * NW], start=True, stop=True)
            mm.then_inc(S.norm, 1)
            pe_up(pe, S, 1, 1, 1, (S.B, 1))

            def ups(j):
                pe_up(pe, S, slot_of(0), 6 * j + 2, 0, (S.A, 6 * j + 1))
                pe_up(pe, S, slot_of(1), 6 * j + 3, 1, (S.B, 6 * j + 2))

            with pe.Fori(0, LAST) as j:
                ups(j)
                pe_up(pe, S, slot_of(2), 6 * j + 4, 0, (S.A, 6 * j + 2))
                pe_up(pe, S, slot_of(3), 6 * j + 5, 1, (S.B, 6 * j + 3))
                pe_down(pe, S, j, (slot_of(4), slot_of(5)), 6 * j + 8, 6 * j + 3, 6 * j + 4)
            j = LAST
            ups(j)
            pe_down(pe, S, j, (slot_of(2), slot_of(3)), 6 * j + 6, 6 * j + 2, 6 * j + 3, after)

        def pe_conv_tails(pe, S):
            pe.wait_ge(S.ut, 2 * NF)
            for q in range(NF // 2):
                if q >= 2:
                    pe.wait_ge(S.ct, q - 1)
                for i in range(4):
                    mm = pe.transpose(ps[0:CT, 6 + q % 2, i * P:(i + 1) * P], utail[:, 4 * q + i, :], ident[:, :])
                mm.then_inc(S.ct_pe, 1)

        def evac(v, S, u, up, sset, free):
            v.wait_ge(S.up, up)
            nc.vector.tensor_tensor(cols3(u[:, 2:2 + N]), bank3(sset), cols3(rb[:, :]), ALU.mult).then_inc(free, 1)

        def keep_tail(v, S, u, half, f, free, n):
            v.wait_ge(free, n)
            nc.vector.tensor_copy(utail[:, bass.ds(half * NF + f, 1), :].rearrange("p o c -> p (o c)"),
                                  u[:, T:2 + N]).then_inc(S.ut, 1)

        def conv_steps(v, L, S, f):
            def tap(c, u, half, t, own):
                w = cwT[:, bass.ds(f + (L * 3 + t) * 2 * NF + half * NF, 1)]
                if t == 1:
                    v.wait_ge(S.tap, 2 * f + 1 + half)
                else:
                    v.wait_ge(S.conv, 8 * f + own)
                nc.vector.scalar_tensor_tensor(out=c[:, 0:T], in0=u[:, t:t + T], scalar=w, in1=c[:, 0:T],
                                               op0=ALU.mult, op1=ALU.add).then_inc(S.conv, 1)
                if t == 0:
                    v.wait_ge(S.conv, 8 * f + own + 1)
                h = convh[:, bass.ds(f + half * NF, 1), L * 2 * NS + t:(L + 1) * 2 * NS:2].rearrange("p o s -> p (o s)")
                nc.vector.scalar_tensor_tensor(out=c[:, T:N], in0=h, scalar=w, in1=c[:, T:N],
                                               op0=ALU.mult, op1=ALU.add).then_inc(S.conv, 1)

            def prod():
                v.wait_ge(S.silu, f + 1)
                v.wait_ge(S.conv, 8 * f + 8)
                nc.vector.tensor_tensor(cb[:, :], ca[:, :], cb[:, :], ALU.mult).then_inc(S.prod, 1)
            return [lambda: tap(ca, ua, 0, 1, 0), lambda: tap(cb, ub, 1, 1, 0),
                    lambda: tap(ca, ua, 0, 0, 1), lambda: tap(cb, ub, 1, 0, 3), prod]

        def dve_gl(v, S, f, c):
            v.wait_ge(S.gh, f + 1)
            nc.vector.tensor_tensor(gl[:, c, :], cb[:, :], gh[:, c, :].bitcast(F32), ALU.subtract).then_inc(S.gl, 1)

        def add_x(v, S, d, down):
            v.wait_ge(S.down, down)
            nc.vector.tensor_tensor(cols3(x[:, d, :]), cols3(x[:, d, :]), bank3(d % 2),
                                    ALU.add).then_inc(S.A if d % 2 == 0 else S.B, 1)

        def dve_ffn_slab0(v, S):
            dve_slab(v, S, 0, -2)

        def dve_ffn(v, L, S, finish):
            dve_slab(v, S, 0, -1)
            dve_slab(v, S, 0, 0)
            m, y = sq[:, 0, 0:N], sq[:, 1, 0:N]
            v.wait_ge(S.norm, 1)
            nc.vector.tensor_scalar(cols3(m), bank3(1), 1.0 / D, EPS, ALU.mult, ALU.add).then_inc(S.B, 1)
            v.wait_ge(S.ra, 1)
            nc.vector.reciprocal(rb[:, :], y).then_inc(S.r, 1)
            v.wait_ge(S.r, 1)
            nc.vector.tensor_tensor(y, rb[:, :], rb[:, :], ALU.mult).then_inc(S.r, 1)
            v.wait_ge(S.r, 2)
            nc.vector.scalar_tensor_tensor(out=m, in0=y, scalar=-0.5, in1=m, op0=ALU.mult, op1=ALU.mult).then_inc(S.r, 1)
            v.wait_ge(S.r, 3)
            nc.vector.scalar_tensor_tensor(out=rb[:, :], in0=m, scalar=1.5, in1=rb[:, :], op0=ALU.add,
                                           op1=ALU.mult).then_inc(S.r, 1)
            v.wait_ge(S.r, 4)
            nc.vector.memset(ua[:, 0:2], 0.0).then_inc(S.r, 1)
            nc.vector.memset(ub[:, 0:2], 0.0).then_inc(S.r, 1)
            v.wait_ge(S.r, 6)
            evac(v, S, ua, 1, 0, S.A)
            keep_tail(v, S, ua, 0, 0, S.A, 1)
            evac(v, S, ub, 2, 1, S.B)
            keep_tail(v, S, ub, 1, 0, S.B, 2)
            for step in conv_steps(v, L, S, 0):
                step()

            def body(j, last):
                dve_slab(v, S, j, 1)
                dve_slab(v, S, j, 2)
                dve_gl(v, S, 2 * j, 0)
                evac(v, S, ua, 4 * j + 3, 0, S.A)
                dve_slab(v, S, j, 3)
                keep_tail(v, S, ua, 0, 2 * j + 1, S.A, 6 * j + 2)
                evac(v, S, ub, 4 * j + 4, 1, S.B)
                if not last:
                    dve_slab(v, S, j, 4)
                keep_tail(v, S, ub, 1, 2 * j + 1, S.B, 6 * j + 3)
                for step in conv_steps(v, L, S, 2 * j + 1):
                    step()
                dve_gl(v, S, 2 * j + 1, 1)
                if last:
                    return
                evac(v, S, ua, 4 * j + 5, 0, S.A)
                dve_slab(v, S, j, 5)
                keep_tail(v, S, ua, 0, 2 * j + 2, S.A, 6 * j + 3)
                evac(v, S, ub, 4 * j + 6, 1, S.B)
                dve_slab(v, S, j, 6)
                keep_tail(v, S, ub, 1, 2 * j + 2, S.B, 6 * j + 4)
                steps = conv_steps(v, L, S, 2 * j + 2)
                for d in range(KC):
                    add_x(v, S, d, 8 * j + d + 1)
                    if d < len(steps):
                        steps[d]()

            with v.Fori(0, LAST) as j:
                body(j, False)
            body(LAST, True)
            for d in range(KC):
                add_x(v, S, d, 8 * LAST + d + 1)
                finish(v, d)

        def act_tap(act, L, S, f, c, u, half, free, n):
            act.wait_ge(free, n)
            wait(act, S.gl, f)
            nc.scalar.activation(c[:, :], u[:, 2:2 + N], ACT.Identity,
                                 bias=cbT[:, bass.ds(f + L * 2 * NF + half * NF, 1)],
                                 scale=cwT[:, bass.ds(f + (L * 3 + 2) * 2 * NF + half * NF, 1)]).then_inc(S.tap, 1)

        def act_silu(act, S, f):
            act.wait_ge(S.conv, 8 * f + 6)
            nc.scalar.activation(ca[:, :], ca[:, :], ACT.Silu).then_inc(S.silu, 1)

        def act_gh(act, S, f, c, down):
            act.wait_ge(S.prod, f + 1)
            wait(act, S.down, down)
            nc.scalar.activation(gh[:, c, :], cb[:, :], ACT.Copy).then_inc(S.gh, 1)

        def act_ffn_slab0(act, S, free):
            act_slab(act, S, 0, -2, free)

        def act_ffn(act, L, S, free12):
            act_slab(act, S, 0, -1, free12)
            act_slab(act, S, 0, 0, free12)
            act.wait_ge(S.B, 1)
            nc.scalar.activation(sq[:, 1, 0:N], sq[:, 0, 0:N], ACT.Sqrt).then_inc(S.ra, 1)
            act_tap(act, L, S, 0, ca, ua, 0, S.A, 1)
            act_tap(act, L, S, 0, cb, ub, 1, S.B, 2)
            act_silu(act, S, 0)

            def body(j, last):
                act_slab(act, S, j, 1, [(S.up, 4 * j + 1), (S.down, 8 * j)])
                act_slab(act, S, j, 2, [(S.up, 4 * j + 2), (S.down, 8 * j)])
                act_gh(act, S, 2 * j, 0, 8 * j)
                act_slab(act, S, j, 3, [(S.up, 4 * j + 3)])
                act_tap(act, L, S, 2 * j + 1, ca, ua, 0, S.A, 6 * j + 2)
                if not last:
                    act_slab(act, S, j, 4, [(S.up, 4 * j + 4)])
                act_tap(act, L, S, 2 * j + 1, cb, ub, 1, S.B, 6 * j + 3)
                act_silu(act, S, 2 * j + 1)
                act_gh(act, S, 2 * j + 1, 1, 8 * j)
                if last:
                    return
                act_slab(act, S, j, 5, [(S.up, 4 * j + 5)])
                act_tap(act, L, S, 2 * j + 2, ca, ua, 0, S.A, 6 * j + 3)
                act_slab(act, S, j, 6, [(S.up, 4 * j + 6)])
                act_tap(act, L, S, 2 * j + 2, cb, ub, 1, S.B, 6 * j + 4)
                act_silu(act, S, 2 * j + 2)

            with act.Fori(0, LAST) as j:
                body(j, False)
            body(LAST, True)

        def added(S, d):
            def ready(e):
                e.wait_ge(*((S.A, 6 * LAST + 3 + d // 2) if d % 2 == 0 else (S.B, 6 * LAST + 4 + d // 2)))
            return ready

        def act_conv_tails(act, L, S):
            for q in range(NF // 2):
                act.wait_ge(S.ct_pe, q + 1)
                if q >= 2 or L:
                    act.wait_ge(ct_out[q % 2], S.ct_out[q % 2] + 32 * (q // 2))
                nc.scalar.activation(ctm[:, q % 2, :], ps[0:CT, 6 + q % 2, :], ACT.Copy).then_inc(S.ct, 1)
                act.wait_ge(S.ct, q + 1)
                cols = slice(q * 512, (q + 1) * 512)
                act.dma_start(o["conv_prompt"][L, 0][:, cols], ctm[0:2, q % 2, :]).then_inc(ct_out[q % 2], 16)
                act.dma_start(o["conv_sample"][L, :, 1, cols], ctm[2:CT, q % 2, :]).then_inc(ct_out[q % 2], 16)

        MT = [P] * 8 + [NS]
        K0 = 6

        def pj_src(u, half, part, g):
            cols = slice(half * HW, (half + 1) * HW)
            if u == 2:
                w = a["w_q"][0].rearrange("(k p) (g n) -> g p k n", p=P, g=GROUPS)
            else:
                w = a["w_kv"].rearrange("(k p) (c g n) -> c g p k n", p=P, c=2, g=GROUPS)[u]
            return w[bass.ds(g, 1), :, 4 * part:4 * part + 4, cols].rearrange("o p k n -> p (o k) n")

        def sp_project(sp):
            S = ffn[0]
            sp.wait_ge(S.gl, NF)
            sp.wait_ge(S.hi, 6 * NB)
            sp.wait_ge(S.lo, 6 * NB)
            sp.dma_start(rot[:, :, :, :], a["rot"]).then_inc(in_rot, 16)
            sp.dma_start(hg[:, 0, :], a["k_gain"].partition_broadcast(P)).then_inc(in_rot, 16)
            sp.dma_start(hg[:, 1, :], a["q_gain"][0].partition_broadcast(P)).then_inc(in_rot, 16)
            with sp.Fori(0, GROUPS) as g:
                def load(m):
                    if m >= 12:
                        return
                    if m < 3:
                        wait(sp, pj_h, 12 * g)
                        wait(sp, pj_l, 12 * g)
                    else:
                        sp.wait_ge(pj_h, 12 * g + m - 2)
                        sp.wait_ge(pj_l, 12 * g + m - 2)
                    sp.dma_start(stage[:, m % 3, :].rearrange("p (k n) -> p k n", k=4),
                                 pj_src(m // 4, m % 4 // 2, m % 2, g)).then_inc(piece_in[m % 3], 16)
                for m in range(7):
                    load(m)
                for u in range(3):
                    for t in range(9):
                        G = 27 * g + 9 * u + t
                        M = MT[t]
                        if u == 1:
                            sp.wait_ge(pj_v, G + (K0 + 1))
                        else:
                            sp.wait_ge(pj_r, 5 * (18 * g + (9 if u else 0) + t + 1))
                        rows = slice(t * P, t * P + M)
                        dst = qs[bass.ds(g, 1), rows, :] if u == 2 else kvs[bass.ds(g, 1), rows, u, :]
                        sp.dma_start(dst.rearrange("o p n -> (o p) n"), kn[0:M, t % 3, :]).then_inc(rows_out[t % 3], 16)
                        if u < 2 and t in (2, 4):
                            load(4 * u + (7 if t == 2 else 8))
                    if u < 2:
                        load(4 * u + 9)
                        load(4 * u + 10)

        def pj_piece(e, g, m, act):
            u, H, part = m // 4, m // 2, m % 2
            gain = G_ATTN if u == 2 else G_KV
            if act:
                e.wait_ge(piece_in[m % 3], 64 * g + 16 * (m // 3 + 1))
                wait(e, pj_pe, 27 * g + 9 * ((H - 3) // 2 + 2))
            else:
                e.wait_ge(pj_h, 12 * g + m + 1)
            for i in range(4):
                k = 4 * part + i
                w = stage[:, m % 3, i * HW:(i + 1) * HW]
                sc_ = gT[:, gain + k:gain + k + 1]
                if act:
                    ins = nc.scalar.activation(wph[H % 3][:, k, :], w, ACT.Copy, scale=sc_)
                else:
                    ins = nc.vector.scalar_tensor_tensor(out=wpl[H % 3][:, k, :], in0=w, scalar=sc_,
                                                         in1=wph[H % 3][:, k, :].bitcast(F32), op0=ALU.mult, op1=ALU.subtract)
            ins.then_inc(pj_h if act else pj_l, 1)

        def pieces_after(u, t):
            if u == 2:
                return []
            return {2: [4 * u + 4], 4: [4 * u + 5], 8: [4 * u + 6, 4 * u + 7]}.get(t, [])

        def act_project(act):
            act.wait_ge(pj_v, 2)
            nc.scalar.activation(rtok[:, :], rtmp[:, 0, :], ACT.Sqrt).then_inc(pj_a, 1)
            act.wait_ge(ffn[0].gl, NF)
            with act.Fori(0, GROUPS) as g:
                for m in range(4):
                    pj_piece(act, g, m, True)
                for u in range(3):
                    for t in range(9):
                        M, G = MT[t], 27 * g + 9 * u + t
                        if u != 1:
                            Q = 18 * g + (9 if u else 0) + t
                            act.wait_ge(pj_pe, G + 10)
                            act.wait_ge(pj_v, K0)
                            wait(act, pj_s, 7 * Q)
                            nc.scalar.activation(sq[0:M, 0, 0:QW], ps[0:M, t % 3, :], ACT.Square,
                                                 scale=rtok[0:M, t:t + 1]).then_inc(pj_sq, 1)
                            act.wait_ge(pj_s, 7 * Q + 2)
                            nc.scalar.activation(hs[0:M, 2, :], hs[0:M, 1, :], ACT.Sqrt).then_inc(pj_rt, 1)
                        for m in pieces_after(u, t):
                            pj_piece(act, g, m, True)

        def dve_project(v):
            v.wait_ge(pj_pe, 9)
            nc.vector.tensor_scalar(rtmp[:, 0, 0:8], ps[:, 7, 0:8], 1.0 / D, EPS, ALU.mult, ALU.add).then_inc(pj_v, 1)
            nc.vector.tensor_scalar(rtmp[0:NS, 0, 8:9], ps[0:NS, 7, 8:9], 1.0 / D, EPS, ALU.mult, ALU.add).then_inc(pj_v, 1)
            newton(v, rtmp[:, 0, :], rtok[:, :], rtmp[:, 2, :], pj_v, 2, pj_a, 1)
            with v.Fori(0, GROUPS) as g:
                for m in range(4):
                    pj_piece(v, g, m, False)
                for u in range(3):
                    for t in range(9):
                        M, G = MT[t], 27 * g + 9 * u + t
                        b = t % 3
                        wait(v, rows_out[b], 144 * g + 16 * (3 * u + t // 3))
                        if u == 1:
                            v.wait_ge(pj_pe, G + 10)
                            nc.vector.tensor_scalar(kn[0:M, b, :], ps[0:M, b, :], rtok[0:M, t:t + 1], None,
                                                    ALU.mult).then_inc(pj_v, 1)
                        else:
                            Q = 18 * g + (9 if u else 0) + t
                            ms, m_, y, tt, f = (hs[0:M, i, :] for i in range(5))
                            v.wait_ge(pj_sq, Q + 1)
                            nc.vector.tensor_reduce(ms, sq[0:M, 0, 0:QW].rearrange("p (h e) -> p h e", h=HEADS), AX.X,
                                                    ALU.add).then_inc(pj_s, 1)
                            v.wait_ge(pj_s, 7 * Q + 1)
                            nc.vector.tensor_scalar(m_, ms, 1.0 / HD, EPS, ALU.mult, ALU.add).then_inc(pj_s, 1)
                            newton(v, m_, y, tt, pj_s, 7 * Q + 2, pj_rt, Q + 1)
                            nc.vector.tensor_scalar(f, y, rtok[0:M, t:t + 1], 0.125 if u else 1.0, ALU.mult,
                                                    ALU.mult).then_inc(pj_s, 1)
                            v.wait_ge(pj_s, 7 * Q + 7)
                            nc.vector.tensor_tensor(kn[0:M, b, :].rearrange("p (h e) -> p h e", h=HEADS),
                                                    ps[0:M, b, :].rearrange("p (h e) -> p h e", h=HEADS),
                                                    f.unsqueeze(2).to_broadcast([M, HEADS, HD]), ALU.mult).then_inc(pj_v, 1)
                        for m in pieces_after(u, t):
                            pj_piece(v, g, m, False)

        def pool_project(q):
            q.wait_ge(in_rot, 48)
            half = HEADS * 8
            with q.Fori(0, GROUPS) as g:
                for u in (0, 2):
                    for t in range(9):
                        M, G, b = MT[t], 27 * g + 9 * u + t, t % 3
                        n = 5 * (18 * g + (9 if u else 0) + t)
                        row = kn[0:M, b, :].rearrange("p (h e) -> p h e", h=HEADS)
                        t1 = sq[0:M, 1, 0:2 * half].rearrange("p (h e) -> p h e", h=HEADS)
                        t2 = sq[0:M, 1, 2 * half:4 * half].rearrange("p (h e) -> p h e", h=HEADS)

                        def per_head(tab, w):
                            return tab.unsqueeze(1).to_broadcast([M, HEADS, w])
                        q.wait_ge(pj_v, G + (K0 + 1))
                        nc.gpsimd.tensor_tensor(row, row, per_head(hg[0:M, 1 if u else 0, :], HD), ALU.mult).then_inc(pj_r, 1)
                        q.wait_ge(pj_r, n + 1)
                        nc.gpsimd.tensor_tensor(t1, row[:, :, 0:16], per_head(rot[0:M, 0, t, :], 16), ALU.mult).then_inc(pj_r, 1)
                        nc.gpsimd.tensor_tensor(t2[:, :, 0:8], row[:, :, 8:16], per_head(rot[0:M, 1, t, 0:8], 8),
                                                ALU.mult).then_inc(pj_r, 1)
                        nc.gpsimd.tensor_tensor(t2[:, :, 8:16], row[:, :, 0:8], per_head(rot[0:M, 1, t, 8:16], 8),
                                                ALU.mult).then_inc(pj_r, 1)
                        q.wait_ge(pj_r, n + 4)
                        nc.gpsimd.tensor_tensor(row[:, :, 0:16], t1, t2, ALU.add).then_inc(pj_r, 1)

        def pe_project(pe):
            pe.wait_ge(split_acc, split[1].acc + KC - 1)
            pe.wait_ge(ffn[0].ct, NF // 2)
            for t in range(9):
                pe.matmul(ps[0:MT[t], 7, t:t + 1], acc[:, t * P:t * P + MT[t]], ones[:, 0:1],
                          start=True, stop=True).then_inc(pj_pe, 1)
            pe.wait_ge(split_lo, split[1].lo + KC)
            with pe.Fori(0, GROUPS) as g:
                for u in range(3):
                    for t in range(9):
                        M, G, tok = MT[t], 27 * g + 9 * u + t, slice(t * P, t * P + MT[t])
                        pe.wait_ge(pj_v, G + (K0 - 2))
                        for h in range(2):
                            W, Wt = wph[(2 * u + h) % 3], wpl[(2 * u + h) % 3]
                            for k in range(KC):
                                if t == 0 and k % 4 == 0:
                                    pe.wait_ge(pj_l, 12 * g + 4 * u + 2 * h + k // 4 + 1)
                                out = ps[0:M, t % 3, h * HW:(h + 1) * HW]
                                pe.matmul(out, xh[:, k, tok], W[:, k, :], start=(k == 0), stop=False)
                                pe.matmul(out, xh[:, k, tok], Wt[:, k, :], start=False, stop=False)
                                mm = pe.matmul(out, xl[:, k, tok], W[:, k, :], start=False, stop=(k == KC - 1))
                        mm.then_inc(pj_pe, 1)

        STEPS = [(0, n, 0, n > 0) for n in range(8)] + [(1, n, r, n > 0) for r in range(4) for n in range(2)] + \
            [(2, s, 0, False) for s in range(8)]
        ROWS = 16 * 9 * GROUPS
        NSTEP, NH = len(STEPS), 2 * len(STEPS)

        def tile_rows(src, s):
            g, n, r, _ = STEPS[s]
            if g == 0:
                return [(slice(0, P), src[n * P:(n + 1) * P, :])]
            if g == 1:
                return [(slice(0, P), src.rearrange("(m r) c -> r m c", r=4)[r, n * P:(n + 1) * P, :])]
            v = src.rearrange("(u r) c -> r u c", r=16)
            return [(slice(64 * e, 64 * e + 64), v[2 * n + e]) for e in range(2)]

        def dmas(s):
            return 2 if STEPS[s][0] == 2 else 1

        def moved(s, ring):
            return 16 * sum(dmas(i) for i in range(s % ring, s + 1, ring))

        def wide(i):
            return STEPS[i // 2][3]

        def span(i):
            return 2 * P if wide(i) else P

        def wides(i):
            return sum(wide(n) for n in range(i + 1))

        KEYS = (P, P, 64)
        CACHES = ("cache_kv_w128", "cache_kv_w512", "cache_kv_w2048")
        ST = 3 * NS
        H_SC, H_NEW, H_SM = 3, 28, 34

        def sp_attention(sp):
            sp.wait_ge(pj_pe, 9 + 27 * GROUPS)
            sp.wait_ge(pj_h, 12 * GROUPS)
            sp.wait_ge(pj_l, 12 * GROUPS)
            for i in range(3):
                sp.wait_ge(rows_out[i], 16 * 9 * GROUPS)

            def load_q(s):
                if s >= 2:
                    sp.wait_ge(at_tp, 2 * s - 3)
                for part, src in tile_rows(qs[STEPS[s][0], 0:T], s):
                    sp.dma_start(qt[part, s % 2, :], src).then_inc(at_q[s % 2], 16)

            def load_kv(s):
                if s >= 4:
                    sp.wait_ge(at_o, 2 * s - 4 if STEPS[s - 3][3] else 2 * s - 6)
                for part, src in tile_rows(kvs[STEPS[s][0], 0:T].rearrange("t c n -> t (c n)"), s):
                    sp.dma_start(kvt[part, s % 4, :], src).then_inc(at_kv[s % 4], 16)

            def load_sample(n):
                s, g = n // 3, n % 3
                if g == 0:
                    if s >= 2:
                        sp.wait_ge(sm_p, n - 3)
                    sp.dma_start(qb[:, s % 2, :, :], qs[:, T + s, :].partition_broadcast(P)).then_inc(sm_q[s % 2], 16)
                if n >= 3:
                    sp.wait_ge(sm_p, n - 2)
                sp.dma_start(kc[0:KEYS[g], n % 3, :], a[CACHES[g]][s, ::DIL[g], 0].rearrange(
                    "t h e -> t (h e)")).then_inc(sm_k[n % 3], 16)

            load_q(0)
            load_kv(0)
            sp.dma_start(maskf[:, :, :], a["masks"]).then_inc(in_rot, 16)
            for g in range(GROUPS):
                sp.dma_start(qn[:, g, :], qs[g, T:N, :]).then_inc(in_new, 16)
                sp.dma_start(stage[0:NS, g, :], kvs[g, T:N].rearrange("t c n -> t (c n)")).then_inc(in_new, 16)
            sp.dma_start(samp[:, :], a["samp"]).then_inc(in_new, 16)
            for s in range(NSTEP + 3):
                if s >= 3:
                    store_o(sp, s - 3)
                if 1 <= s < NSTEP:
                    load_q(s)
                    load_kv(s)
                for n in (2 * s - 4, 2 * s - 3):
                    if 0 <= n < ST:
                        load_sample(n)
                if s == 3:
                    for g, (name, rows) in enumerate((("kv_w128", 128), ("kv_w512", 512), ("kv_w2048", T))):
                        sp.dma_start(o[name + "_prompt"][0].rearrange("t c h e -> t c (h e)"),
                                     kvs[g, T - rows:T]).then_inc(kv_out, 16)
                        sp.dma_start(o[name + "_sample"][:, 0].rearrange("t c h e -> t c (h e)"),
                                     kvs[g, T:N]).then_inc(kv_out, 16)
                if s == 17:
                    sp.wait_ge(sm_p, ST)
                    sp.dma_start(diag, a["diag"]).then_inc(in_diag, 16)
                    for n in range(NV):
                        load_v(sp, n)

        def load_v(e, n):
            s, g = n // 3, n % 3
            if n >= NV:
                e.wait_ge(sm_o, n - NV + 1)
            e.dma_start(vc[0:KEYS[g], n % NV, :], a[CACHES[g]][s, ::DIL[g], 1].rearrange(
                "t h e -> t (h e)")).then_inc(sm_vin[n % NV], 16)

        def store_o(e, s):
            e.wait_ge(at_oc, 2 * s + 2)
            e.wait_ge(at_e, 2 * s + 2)
            for part, dst in tile_rows(os_[STEPS[s][0]], s):
                e.dma_start(dst, osb[part, s % 3, :]).then_inc(rows_out[s % 3], 16)

        def scores_out(i):
            b = 2 * (i % 2)
            return ps[:, b:b + 2, 0:2 * span(i)].rearrange("p b (h n) -> p b h n", h=2)

        def pe_attention(pe):
            def turn(tile, s):
                for hp in range(4):
                    mm = pe.transpose(ps[:, 7, hp * P:(hp + 1) * P], tile[:, hp * P:(hp + 1) * P], ident[:, :])
                mm.then_inc(at_tp, 1)

            def turn_q(s):
                pe.wait_ge(at_q[s % 2], moved(s, 2))
                wait(pe, at_tc, 2 * s)
                turn(qt[:, s % 2, :], s)

            def turn_k(s):
                pe.wait_ge(at_kv[s % 4], moved(s, 4))
                pe.wait_ge(at_tc, 2 * s + 1)
                turn(kvt[:, s % 4, 0:QW], s)

            def scores(i):
                s, half = i // 2, i % 2
                b = 2 * (i % 2)
                pe.wait_ge(at_tc, 2 * s + 2)
                if i >= 2:
                    pe.wait_ge(at_e, i - 1)
                if i == 0:
                    pe.wait_ge(at_mk, 4)
                m = 0 if wide(i) else (2 if STEPS[s][0] == 2 else 1)
                for c in range(2):
                    pe.matmul(ps[:, b + c, 0:2 * span(i)], identb[:, :], mask[:, m, 0:2 * span(i)], start=True, stop=True)
                slots = [(s - 1) % 3, s % 3] if wide(i) else [s % 3]
                for pair in range(2):
                    for w, slot in enumerate(slots):
                        for odd in range(2):
                            part = slice(64 * odd, 64 * odd + 64)
                            hp = 2 * half + pair
                            at = pair * span(i) + w * P
                            mm = pe.matmul(ps[:, b + odd, at:at + P], qT[part, s % 2, hp * P:(hp + 1) * P],
                                           kT[part, slot, hp * P:(hp + 1) * P], start=False, stop=True,
                                           skip_group_check=True)
                mm.then_inc(at_s, 1)

            def turn_p(i):
                pe.wait_ge(at_e, i + 1)
                if i:
                    pe.wait_ge(at_pa, i)
                wait(pe, at_pb, wides(i - 1))
                for n in range(8 if wide(i) else 4):
                    mm = pe.transpose(ps[:, 4 + n // 4, n % 4 * P:(n % 4 + 1) * P], prob[:, i % 2, n * P:(n + 1) * P],
                                      ident[:, :])
                mm.then_inc(at_pt, 1)

            def outputs(i):
                s = i // 2
                pe.wait_ge(at_pa, i + 1)
                wait(pe, at_pb, wides(i))
                if i:
                    pe.wait_ge(at_oc, i)
                for j in range(4):
                    h = 4 * (i % 2) + j
                    tiles = [(s - 1) % 4, s % 4] if wide(i) else [s % 4]
                    for w, slot in enumerate(tiles):
                        n = j * len(tiles) + w
                        v = kvt[:, slot, QW + h // 2 * P:QW + (h // 2 + 1) * P]
                        mm = pe.matmul(ps[:, 6, j * P:(j + 1) * P], probT[:, i % 2, n * P:(n + 1) * P], v,
                                       start=(w == 0), stop=(w == len(tiles) - 1))
                mm.then_inc(at_o, 1)

            turn_q(0)
            turn_k(0)
            for i in range(NH + 2):
                if i < NH:
                    scores(i)
                if i // 2 + 1 < NSTEP:
                    (turn_k if i % 2 else turn_q)(i // 2 + 1)
                if 0 < i <= NH:
                    turn_p(i - 1)
                if i >= 2:
                    outputs(i - 2)
                if i == H_SM:
                    pe.wait_ge(at_pb, wides(NH - 1))
                    pe.wait_ge(sm_r, ST)
                    pe.wait_ge(sm_new, 9)
                    for g in range(GROUPS):
                        pe.transpose(ps[0:64, 5, g * P:g * P + KEYS[g]], sc[0:KEYS[g], g * 64:(g + 1) * 64],
                                     ident[0:KEYS[g], 0:KEYS[g]])
                    for g in range(GROUPS):
                        mm = pe.matmul(ps[0:64, 5, SK - 3 + g:SK - 2 + g], bnew[:, g * 64:(g + 1) * 64], ones[0:NS, 0:1],
                                       start=True, stop=True)
                    mm.then_inc(sm_pe, 1)
                if i == H_SM + 2:
                    pe.wait_ge(sm_st, 3)
                    for g in range(GROUPS):
                        mm = pe.transpose(ps[0:KEYS[g], 5, g * 64:(g + 1) * 64], sall[:, g * P:g * P + KEYS[g]],
                                          ident[0:64, 0:64])
                    mm.then_inc(sm_pe, 1)
                    pe.wait_ge(sm_st, 4)
                    pe.matmul(ps[0:NS, 5, 448:472], sel8, an, start=True, stop=True).then_inc(sm_pe, 1)

        def dve_attention(v):
            v.wait_ge(in_rot, 16 * 4)
            nc.vector.tensor_copy(identb[:, :], ident[:, :]).then_inc(at_mk, 1)
            for m in range(3):
                if m == 0:
                    ins = nc.vector.tensor_copy(mask[:, 0, :].rearrange("p (w n) -> p w n", w=2),
                                                maskf[:, 0:2, :].rearrange("p c n -> p (c n)").unsqueeze(1).to_broadcast([P, 2, 2 * P]))
                else:
                    ins = nc.vector.tensor_copy(mask[:, m, 0:2 * P].rearrange("p (w n) -> p w n", w=2),
                                                maskf[:, m, :].unsqueeze(1).to_broadcast([P, 2, P]))
                ins.then_inc(at_mk, 1)

            def turned(s, k):
                v.wait_ge(at_tp, 2 * s + 1 + k)
                nc.vector.tensor_copy(kT[:, s % 3, :] if k else qT[:, s % 2, :], ps[:, 7, :]).then_inc(at_tc, 1)

            def maxima(i):
                s = i // 2
                v.wait_ge(at_s, i + 1)
                if s >= 3:
                    v.wait_ge(rows_out[s % 3], ROWS + moved(s - 3, 3))
                dst = osb[:, s % 3, QW + 4 * (i % 2):QW + 4 * (i % 2) + 4].rearrange("p (h b) -> p b h", b=2)
                nc.vector.tensor_reduce(dst, scores_out(i), AX.X, ALU.max, negate=True).then_inc(at_m, 1)

            def probs(i):
                v.wait_ge(at_pt, i + 1)
                nc.vector.tensor_copy(probT[:, i % 2, 0:512], ps[:, 4, :]).then_inc(at_pa, 1)

            def outs(i):
                v.wait_ge(at_o, i + 1)
                src = ps[:, 6, :].rearrange("p (q o) -> p q o", q=2)
                dst = osb[:, i // 2 % 3, 256 * (i % 2):256 * (i % 2) + 256].rearrange("p (q o) -> p q o", q=2)
                nc.vector.tensor_copy(dst[:, :, 0:64], src[:, :, 0:64])
                nc.vector.tensor_copy(dst[:, :, 64:128], src[:, :, 192:256]).then_inc(at_oc, 1)

            turned(0, 0)
            turned(0, 1)
            for i in range(NH + 2):
                if i < NH:
                    maxima(i)
                if i // 2 + 1 < NSTEP:
                    turned(i // 2 + 1, i % 2)
                if 0 < i <= NH:
                    probs(i - 1)
                if i >= 2:
                    outs(i - 2)
                if 0 <= i - H_SC < ST:
                    n = i - H_SC
                    s, g = n // 3, n % 3
                    v.wait_ge(sm_p, n + 1)
                    nc.vector.tensor_reduce(sc[0:KEYS[g], g * 64 + s * 8:g * 64 + s * 8 + 8],
                                            prod[0:KEYS[g], 0, :].rearrange("p (h e) -> p h e", h=HEADS), AX.X,
                                            ALU.add).then_inc(sm_r, 1)
                if i == H_NEW:
                    dve_new_keys(v)
                if i == H_SM:
                    v.wait_ge(sm_pe, 1)
                    nc.vector.tensor_reduce(stat[:, 0:1], ps[0:64, 5, 0:SK], AX.X, ALU.max, negate=True).then_inc(sm_st, 1)
                if i == H_SM + 1:
                    v.wait_ge(sm_e, 1)
                    nc.vector.reciprocal(stat[:, 2:3], stat[:, 1:2]).then_inc(sm_st, 1)
                    v.wait_ge(sm_st, 2)
                    nc.vector.tensor_scalar(sall, sall, stat[:, 2:3], None, ALU.mult).then_inc(sm_st, 1)
                    v.wait_ge(sm_st, 3)
                    nc.vector.tensor_tensor(an.rearrange("p (g h) -> p g h", g=GROUPS),
                                            del8.unsqueeze(1).to_broadcast([64, GROUPS, HEADS]),
                                            sall[:, SK - 3:SK].unsqueeze(2).to_broadcast([64, GROUPS, HEADS]),
                                            ALU.mult).then_inc(sm_st, 1)
                if i == H_SM + 2:
                    dve_sample_probs(v)

        def dve_new_keys(v):
            v.wait_ge(in_new, 16 * 7)
            v.wait_ge(sm_z, 1)
            tmp = om1[0:NS, :]
            for g in range(GROUPS):
                wait(v, sm_new, 2 * g)
                nc.vector.tensor_tensor(tmp, qn[:, g, :], stage[0:NS, g, 0:QW], ALU.mult).then_inc(sm_new, 1)
                v.wait_ge(sm_new, 2 * g + 1)
                nc.vector.tensor_reduce(snew[:, g * 8:g * 8 + 8], tmp.rearrange("p (h e) -> p h e", h=HEADS), AX.X,
                                        ALU.add).then_inc(sm_new, 1)
            v.wait_ge(sm_new, 6)
            for g in range(GROUPS):
                nc.vector.tensor_tensor(bnew[:, g * 64:(g + 1) * 64].rearrange("p (s h) -> p s h", s=NS),
                                        del64.rearrange("p (s h) -> p s h", s=NS),
                                        snew[:, g * 8:g * 8 + 8].unsqueeze(1).to_broadcast([NS, NS, HEADS]),
                                        ALU.mult).then_inc(sm_new, 1)

        def dve_sample_probs(v):
            v.wait_ge(sm_pe, 3)
            v.wait_ge(sm_z, 1)
            for part, g0, g1 in ((P, 0, 2), (64, 2, 3)):
                nc.vector.tensor_copy(pT[0:part, g0 * 256:g1 * 256].rearrange("p (s w) -> p s w", w=32)[:, :, 0:HEADS],
                                      ps[0:part, 5, g0 * 64:g1 * 64].rearrange("p (s w) -> p s w", w=HEADS)).then_inc(sm_st, 1)
            nc.vector.tensor_copy(pnew, ps[0:NS, 5, 448:472]).then_inc(sm_st, 1)
            v.wait_ge(sm_st, 7)

            def part(dst, g):
                nc.vector.tensor_tensor(dst.rearrange("p (h e) -> p h e", h=HEADS),
                                        stage[0:NS, g, QW:2 * QW].rearrange("p (h e) -> p h e", h=HEADS),
                                        pnew[:, g * 8:g * 8 + 8].unsqueeze(2).to_broadcast([NS, HEADS, HD]),
                                        ALU.mult).then_inc(sm_st, 1)
            tmp = om1[0:NS, :]
            part(onew, 0)
            for g in range(1, GROUPS):
                part(tmp, g)
                v.wait_ge(sm_st, 7 + 2 * g)
                nc.vector.tensor_tensor(onew, onew, tmp, ALU.add).then_inc(sm_st, 1)
                v.wait_ge(sm_st, 8 + 2 * g)

        def act_attention(act):
            for i in range(NH + 2):
                if i < NH:
                    s, n = i // 2, span(i)
                    act.wait_ge(at_m, i + 1)
                    if i >= 2:
                        act.wait_ge(at_pt, i - 1)
                    src = scores_out(i)
                    for j in range(4):
                        h = 4 * (i % 2) + j
                        ins = nc.scalar.activation(prob[:, i % 2, j * n:(j + 1) * n], src[:, j % 2, j // 2, :], ACT.Exp,
                                                   bias=osb[:, s % 3, QW + h:QW + h + 1],
                                                   accum_out=osb[:, s % 3, QW + HEADS + h:QW + HEADS + h + 1])
                    ins.then_inc(at_e, 1)
                if 0 < i <= NH and wide(i - 1):
                    act.wait_ge(at_pt, i)
                    nc.scalar.activation(probT[:, (i - 1) % 2, 512:1024], ps[:, 5, :], ACT.Copy).then_inc(at_pb, 1)
                if i == H_SM:
                    act.wait_ge(sm_st, 1)
                    nc.scalar.activation(sall, ps[0:64, 5, 0:SK], ACT.Exp, bias=stat[:, 0:1],
                                         accum_out=stat[:, 1:2]).then_inc(sm_e, 1)

        def pool_attention(q):
            q.wait_ge(pj_r, 5 * 18 * GROUPS)
            q.wait_ge(pj_s, 7 * 18 * GROUPS)
            nc.gpsimd.memset(pT, 0.0).then_inc(sm_z, 1)
            for n in range(ST):
                s, g = n // 3, n % 3
                if g == 0:
                    q.wait_ge(sm_q[s % 2], 16 * (s // 2 + 1))
                q.wait_ge(sm_k[n % 3], 16 * (n // 3 + 1))
                wait(q, sm_r, n)
                nc.gpsimd.tensor_tensor(prod[0:KEYS[g], 0, :], kc[0:KEYS[g], n % 3, :], qb[0:KEYS[g], s % 2, g, :],
                                        ALU.mult).then_inc(sm_p, 1)

        MG = 10

        def sp_merge(sp):
            for i in range(3):
                sp.wait_ge(rows_out[i], ROWS + moved(NSTEP - 3 + i, 3))
            sp.wait_ge(at_o, NH)

            def load(t):
                if t >= 2:
                    sp.wait_ge(mg_v, MG * (t - 1))
                sp.dma_start(om[:, t % 2, :, :], os_[:, t * P:(t + 1) * P, :].rearrange("g p c -> p g c")).then_inc(
                    mg_in[t % 2], 16)

            load(0)
            load(1)
            nv = NV
            for t in range(2, 8):
                while nv < min(ST, NV + 4 * (t - 1)):
                    load_v(sp, nv)
                    nv += 1
                load(t)
            assert nv == ST
            for k in range(4):
                if k == 0:
                    sp.wait_ge(sm_st, 12)
                if k == 3:
                    sp.wait_ge(wo_h, 1)
                    sp.wait_ge(wo_l, 1)
                sp.dma_start(stage[:, k % 3, :], a["w_o"][0, k * P:(k + 1) * P, :]).then_inc(piece_in[k % 3], 16)

        def dve_merge(v):
            def first(t):
                b = t % 2
                nm = om[:, b, :, QW:QW + HEADS]
                v.wait_ge(mg_in[b], 16 * (t // 2 + 1))
                if t >= 2:
                    v.wait_ge(mg_p, t - 1)
                    v.wait_ge(mg_v, MG * (t - 1))
                nc.vector.tensor_reduce(ow[:, b, 0, 0:8], nm.rearrange("p g h -> p h g"), AX.X, ALU.min).then_inc(mg_a, 1)
                v.wait_ge(mg_a, 2 * t + 1)
                nc.vector.tensor_tensor(ow[:, b, 1, :].rearrange("p (g h) -> p g h", g=GROUPS),
                                        ow[:, b, 0, 0:8].unsqueeze(1).to_broadcast([P, GROUPS, HEADS]), nm,
                                        ALU.subtract).then_inc(mg_a, 1)

            def weighted(dst, src, w, h=HEADS):
                return dict(out=dst.rearrange("p (h e) -> p h e", h=h), in0=src.rearrange("p (h e) -> p h e", h=h),
                            in1=w.unsqueeze(2).to_broadcast([P, h, HD]), op=ALU.mult)

            def second(t):
                b, n = t % 2, MG * t
                den = om[:, b, :, QW + HEADS:OW]
                three_g = dict(g=GROUPS)
                e, ed, w = (ow[:, b, i, :] for i in (1, 2, 3))
                v.wait_ge(mg_e, t + 1)
                nc.vector.tensor_tensor(ed.rearrange("p (g h) -> p g h", **three_g), e.rearrange("p (g h) -> p g h", **three_g),
                                        den, ALU.mult).then_inc(mg_v, 1)
                v.wait_ge(mg_v, n + 1)
                nc.vector.tensor_reduce(ow[:, b, 0, 8:16], ed.rearrange("p (g h) -> p h g", **three_g), AX.X,
                                        ALU.add).then_inc(mg_v, 1)
                v.wait_ge(mg_v, n + 2)
                nc.vector.reciprocal(ow[:, b, 0, 16:24], ow[:, b, 0, 8:16]).then_inc(mg_v, 1)
                v.wait_ge(mg_v, n + 3)
                nc.vector.tensor_tensor(w.rearrange("p (g h) -> p g h", **three_g), e.rearrange("p (g h) -> p g h", **three_g),
                                        ow[:, b, 0, 16:24].unsqueeze(1).to_broadcast([P, GROUPS, HEADS]),
                                        ALU.mult).then_inc(mg_v, 1)
                v.wait_ge(mg_v, n + 4)
                if t >= 2:
                    v.wait_ge(mg_pe, t - 1)
                nc.vector.tensor_tensor(**weighted(ot[:, b, 0, :], om[:, b, 0, 0:QW], w[:, 0:8])).then_inc(mg_v, 1)
                nc.vector.tensor_tensor(**weighted(ot[:, b, 1, :], om[:, b, 2, 0:QW], w[:, 16:24])).then_inc(mg_v, 1)

            def third(t):
                b, n = t % 2, MG * t
                v.wait_ge(mg_v, n + 6)
                nc.vector.tensor_tensor(ot[:, b, 0, :], ot[:, b, 0, :], ot[:, b, 1, :], ALU.add).then_inc(mg_v, 1)
                v.wait_ge(mg_v, n + 7)
                v.wait_ge(mg_p, t + 1)
                nc.vector.tensor_tensor(ot[:, b, 0, :], ot[:, b, 0, :], om[:, b, 1, 0:QW], ALU.add).then_inc(mg_v, MG - 7)

            def lo(t):
                v.wait_ge(mg_h, t + 1)
                nc.vector.tensor_tensor(oTl[:, :, t * P:(t + 1) * P], ps[:, 6 + t % 2, :].rearrange("p (c n) -> p c n", c=4),
                                        oTh[:, :, t * P:(t + 1) * P].bitcast(F32), ALU.subtract).then_inc(mg_l, 1)

            def split_wo(k):
                v.wait_ge(wo_h, k + 1)
                nc.vector.tensor_tensor(wol[:, k, :], stage[:, k % 3, :], woh[:, k, :].bitcast(F32), ALU.subtract).then_inc(wo_l, 1)

            first(0)
            for t in range(8):
                if t < 7:
                    first(t + 1)
                second(t)
                if t:
                    lo(t - 1)
                third(t)
                if t in (3, 6):
                    i = t // 3 - 1
                    if i == 0:
                        v.wait_ge(in_diag, 16)
                        v.wait_ge(sm_st, 12)
                    v.wait_ge(sm_o, 12 * (i + 1))
                    nc.vector.tensor_tensor((om1, om2)[i], ps[:, 1 + 2 * i, :], diag, ALU.mult).then_inc(sm_st, 1)
            lo(7)
            v.wait_ge(sm_fh, 1)
            nc.vector.tensor_tensor(oTl[:, :, T:N], ps[:, 5, 0:4 * NS].rearrange("p (c s) -> p c s", c=4),
                                    oTh[:, :, T:N].bitcast(F32), ALU.subtract).then_inc(sm_fl, 1)
            for k in range(4):
                split_wo(k)
            for d in range(KC):
                v.wait_ge(wo_pe, d + 1)
                nc.vector.tensor_tensor(cols3(x[:, d, :]), cols3(x[:, d, :]), bank3(d % 2), ALU.add).then_inc(wo_x, 1)
                if d:
                    dve_split(v, split[2], d - 1, G_FFN + KC)
            dve_split(v, split[2], KC - 1, G_FFN + KC)
            dve_ffn_slab0(v, ffn[1])

        def pool_merge(q):
            for t in range(8):
                b = t % 2
                q.wait_ge(mg_v, MG * t + 4)
                row = om[:, b, 1, 0:QW].rearrange("p (h e) -> p h e", h=HEADS)
                nc.gpsimd.tensor_tensor(row, row, ow[:, b, 3, 8:16].unsqueeze(2).to_broadcast([P, HEADS, HD]),
                                        ALU.mult).then_inc(mg_p, 1)

        def act_merge(act):
            def exps(t):
                b = t % 2
                act.wait_ge(mg_a, 2 * t + 2)
                nc.scalar.activation(ow[:, b, 1, :], ow[:, b, 1, :], ACT.Exp).then_inc(mg_e, 1)

            def hi(t):
                act.wait_ge(mg_pe, t + 1)
                nc.scalar.activation(oTh[:, :, t * P:(t + 1) * P], ps[:, 6 + t % 2, :].rearrange("p (c n) -> p c n", c=4),
                                     ACT.Copy).then_inc(mg_h, 1)
            for t in range(8):
                exps(t)
                if t:
                    hi(t - 1)
            hi(7)
            act.wait_ge(sm_f, 1)
            nc.scalar.activation(oTh[:, :, T:N], ps[:, 5, 0:4 * NS].rearrange("p (c s) -> p c s", c=4),
                                 ACT.Copy).then_inc(sm_fh, 1)
            act.wait_ge(sm_o, ST)
            for k in range(4):
                act.wait_ge(piece_in[k % 3], 64 * GROUPS + 16 * (k // 3 + 1))
                nc.scalar.activation(woh[:, k, :], stage[:, k % 3, :], ACT.Copy).then_inc(wo_h, 1)
            act.wait_ge(wo_l, 4)
            for d in range(KC):
                act.wait_ge(wo_x, d + 1)
                act_split(act, split[2], d, G_FFN + KC)
            act_ffn_slab0(act, ffn[1], [(wo_pe, KC)])

        def pe_merge(pe):
            def turn(t):
                pe.wait_ge(mg_v, MG * (t + 1))
                if t >= 2:
                    pe.wait_ge(mg_l, t - 1)
                for c in range(4):
                    mm = pe.transpose(ps[:, 6 + t % 2, c * P:(c + 1) * P], ot[:, t % 2, 0, c * P:(c + 1) * P], ident[:, :])
                mm.then_inc(mg_pe, 1)

            def values(n):
                s, g = n // 3, n % 3
                pe.wait_ge(sm_vin[n % NV], 16 * (n // NV + 1))
                if n == 0:
                    pe.wait_ge(sm_st, 6)
                pe.matmul(ps[32 * (s % 4):32 * (s % 4) + 32, 1 + 2 * (s // 4), :],
                          pT[0:KEYS[g], (g * NS + s) * 32:(g * NS + s + 1) * 32], vc[0:KEYS[g], n % NV, :],
                          start=(g == 0), stop=(g == GROUPS - 1), tile_position=(0, 32 * (s % 4))).then_inc(sm_o, 1)

            pe.wait_ge(at_e, NH)
            pe.wait_ge(at_oc, NH)
            for t in range(8):
                if t < 7:
                    for n in range(4 * t, min(4 * t + 4, ST)):
                        values(n)
                turn(t)
            pe.wait_ge(sm_st, 14)
            for c in range(4):
                cols = slice(c * P, (c + 1) * P)
                for i, m in enumerate((om1, om2)):
                    out = ps[:, 5, c * NS + 4 * i:c * NS + 4 * i + 4]
                    pe.matmul(out, m[:, cols], selS, start=True, stop=False)
                    mm = pe.matmul(out, onew[:, cols], ident[0:NS, 4 * i:4 * i + 4], start=False, stop=True)
            mm.then_inc(sm_f, 1)
            pe.wait_ge(mg_l, 8)
            pe.wait_ge(sm_fl, 1)
            pe.wait_ge(wo_l, 4)
            for d in range(KC):
                if d >= 2:
                    pe.wait_ge(wo_x, d - 1)
                parts = []
                for k in range(4):
                    parts += three(woh[:, k, d * P:(d + 1) * P], wol[:, k, d * P:(d + 1) * P], oTh[:, k, :], oTl[:, k, :])
                group(pe, 3 * (d % 2), parts).then_inc(wo_pe, 1)

        def pe_result(pe, d):
            added(ffn[1], d)(pe)
            if d == 0:
                pe.wait_ge(ffn[1].ct, NF // 2)
            else:
                pe.wait_ge(y_a, d)
                pe.wait_ge(y_v, d)
            for t in range(8):
                mm = pe.transpose(ps[:, 6 + t // 4, t % 4 * P:(t % 4 + 1) * P], x[:, d, t * P:(t + 1) * P], ident[:, :])
            mm.then_inc(y_pe, 1)

        def copy_result(e, d, h):
            e.wait_ge(y_pe, d + 1)
            if d >= 2:
                e.wait_ge(mg_in[d % 2], 64 + 16 * (d // 2))
            dst, src = yst[:, d % 2, 4 * h:4 * h + 4, :].rearrange("p t n -> p (t n)"), ps[:, 6 + h, :]
            if h:
                nc.vector.tensor_copy(dst, src).then_inc(y_v, 1)
            else:
                nc.scalar.activation(dst, src, ACT.Copy).then_inc(y_a, 1)

        def sp_results(sp):
            for d in range(KC):
                sp.wait_ge(y_a, d + 1)
                sp.wait_ge(y_v, d + 1)
                sp.dma_start(o["y_prompt"][0, :, d * P:(d + 1) * P].rearrange("(t p) n -> p t n", p=P),
                             yst[:, d % 2, :, :]).then_inc(mg_in[d % 2], 16)
            sp.wait_ge(y_s, 1)
            sp.dma_start(o["y_sample"][:, 0, :], yss[:, :]).then_inc(ys_out, 16)

        @block.sync
        def _(sp):
            sp_start(sp)

            def begin0(e, n):
                if n == 1:
                    sp_pool_tails(e)
                if n:
                    e.wait_ge(wp_l, 1)
                    e.wait_ge(wp_h, 1)
            sp_ffn(sp, 0, ffn[0], begin0)
            sp_project(sp)
            sp_attention(sp)
            sp_merge(sp)

            def begin1(e, n):
                e.wait_ge(wo_h, 4)
                e.wait_ge(wo_l, 4)
            sp_ffn(sp, 1, ffn[1], begin1)
            sp_results(sp)
            sp.wait_ge(out_w, 16 * 3)
            sp.wait_ge(tl_out, 32)
            sp.wait_ge(kv_out, 16 * 6)
            sp.wait_ge(ct_out[0], 32 * 6 * DEPTH)
            sp.wait_ge(ct_out[1], 32 * 5 * DEPTH)
            for i in range(2):
                sp.wait_ge(mg_in[i], 64 + 16 * 4)
            sp.wait_ge(ys_out, 16)

        @block.gpsimd
        def _(g):
            pool_start(g)
            pool_split(g, split[1])
            pool_project(g)
            pool_attention(g)
            pool_merge(g)
            pool_split(g, split[2])

        @block.scalar
        def _(act):
            act_start(act)
            act_ffn(act, 0, ffn[0], [(pool_pe, 8)])
            for d in range(KC):
                added(ffn[0], d)(act)
                act_split(act, split[1], d, None)
            act_conv_tails(act, 0, ffn[0])
            act_project(act)
            act_attention(act)
            act_merge(act)
            act_ffn(act, 1, ffn[1], [])
            act_conv_tails(act, 1, ffn[1])
            for d in range(KC):
                copy_result(act, d, 0)

        @block.tensor
        def _(pe):
            pe_start(pe)
            pe_pool(pe)
            pe_ffn(pe, 0, ffn[0], split[0], (pool_x, 7))
            pe_conv_tails(pe, ffn[0])
            pe_project(pe)
            pe_attention(pe)
            pe_merge(pe)

            def after(d):
                if d == 2:
                    pe_conv_tails(pe, ffn[1])
                if d >= 4:
                    pe_result(pe, d - 4)
            pe_ffn(pe, 1, ffn[1], split[2], (wo_x, 7), after)
            for d in range(4, KC):
                pe_result(pe, d)
            for d in range(KC):
                mm = pe.transpose(ps[0:NS, d // 4, d % 4 * P:(d % 4 + 1) * P], x[:, d, T:N], ident[:, :])
            mm.then_inc(y_pe, 1)

        @block.vector
        def _(v):
            dve_start(v)
            dve_ffn(v, 0, ffn[0], lambda e, d: dve_split(e, split[1], d, None))
            dve_project(v)
            dve_attention(v)
            dve_merge(v)

            def finish(e, d):
                if d >= 4:
                    copy_result(e, d - 4, 1)
            dve_ffn(v, 1, ffn[1], finish)
            for d in range(4, KC):
                copy_result(v, d, 1)
            v.wait_ge(y_pe, KC + 1)
            nc.vector.tensor_copy(yss.rearrange("p (b n) -> p b n", b=2), ps[0:NS, 0:2, :]).then_inc(y_s, 1)


def constants():
    ident = np.eye(P, dtype=np.float32)
    sel = np.zeros((NS * HIST, 4, NS), np.float32)
    invc = np.empty((P, 4, PAD), np.float32)
    for w, width in enumerate(WINDOWS):
        for s in range(NS):
            sel[(s + 1) * HIST - (width - 1):(s + 1) * HIST, w, s] = 1
        invc[:, w, :] = 1.0 / np.minimum(np.arange(PAD) + 1, width)
    pos = np.minimum(np.arange(T + P), T).astype(np.float32)
    inv = (np.float32(500000.0) ** (-np.arange(0, 16, 2, dtype=np.float32) / np.float32(16))).astype(np.float32)
    ang = (pos[:, None] * inv[None, :]).astype(np.float32).astype(np.float64)
    c, s = np.cos(ang), np.sin(ang)
    rot = np.stack([np.concatenate([c, c], 1), np.concatenate([-s, s], 1)]).astype(np.float32)
    rot = rot.reshape(2, 9, P, 16).transpose(2, 0, 1, 3)
    q, k = np.arange(P)[:, None], np.arange(P)[None, :]
    masks = np.zeros((P, 3, P), np.float32)
    masks[:, 0][k < q] = NEG
    masks[:, 1][k > q] = NEG
    masks[:, 2][(k > q) | (k // 64 != q // 64)] = NEG
    samp = np.zeros((P, 84), np.float32)
    for s in range(NS):
        for h in range(HEADS):
            samp[32 * (s % 4) + h, s % 4] = 1
            samp[s * HEADS + h, 4 + s] = 1
            samp[s * HEADS + h, 12 + h] = 1
            samp[s, 20 + s * HEADS + h] = 1
    diag = np.zeros((P, QW), np.float32)
    for j in range(4):
        for h in range(HEADS):
            diag[32 * j + h, h * HD:(h + 1) * HD] = 1
    return dict(ident=ident, sel=sel, invc=invc, rot=rot, masks=masks, samp=samp, diag=diag)


_OUTS = {
    "y_prompt": (1, T, D), "y_sample": (NS, 1, D), "pool_prompt": (1, 1, HIST, D), "pool_sample": (1, NS, HIST, D),
    "conv_prompt": (DEPTH, 1, 2, 2 * F), "conv_sample": (DEPTH, NS, 2, 2 * F),
    "kv_w128_prompt": (1, 128, 2, HEADS, HD), "kv_w128_sample": (NS, 1, 2, HEADS, HD),
    "kv_w512_prompt": (1, 512, 2, HEADS, HD), "kv_w512_sample": (NS, 1, 2, HEADS, HD),
    "kv_w2048_prompt": (1, T, 2, HEADS, HD), "kv_w2048_sample": (NS, 1, 2, HEADS, HD),
}


def kernel(**inputs):
    import concourse.bacc as bacc
    from concourse.bass_utils import run_bass_kernel_spmd

    nc = bacc.Bacc("TRN2", target_bir_lowering=False, num_devices=1)
    arrays = {"in_" + name: np.ascontiguousarray(v) for name, v in {**inputs, **constants()}.items()}
    a = {name[3:]: nc.dram_tensor(name, v.shape, mybir.dt.from_np(v.dtype), kind="ExternalInput").ap()
         for name, v in arrays.items()}
    o = {name: nc.dram_tensor("out_" + name, shape, F32, kind="ExternalOutput").ap() for name, shape in _OUTS.items()}
    build(nc, a, o)
    r = run_bass_kernel_spmd(nc, [arrays], core_ids=[0])
    return tuple(r.results[0]["out_" + name] for name in _OUTS)
```

```python
from contextlib import ExitStack

import numpy as np

import concourse.bass as bass
import concourse.mybir as mybir

P = 128
D = 1024
T = 1024
NS = 8
N = T + NS
NC = 3
NW = N // NC
KC = D // P
F = 2816
NF = F // P
NB = NF // 2
LAST = NB - 1
SLABS = 3 * NF
DEPTH = 2
HIST = 15
TAIL = HIST + NS
CT = 2 + NS
PAD = 16
WINDOWS = (2, 4, 8, 16)
GROUPS = 3
HEADS = 8
HD = 64
QW = HEADS * HD
DIL = (1, 4, 16)
HW = QW // 2
OW = QW + 2 * HEADS
SK = 129 + 129 + 65
EPS = 1e-6
NEG = -1e30

F32 = mybir.dt.float32
F32R = mybir.dt.float32r
BF16 = mybir.dt.bfloat16
ALU = mybir.AluOpType
ACT = mybir.ActivationFunctionType
AX = mybir.AxisListType

G_POOL, G_SCALE, G_FFN, G_KV, G_ATTN = 0, KC, 2 * KC, 4 * KC, 5 * KC


def build(nc, a, o):
    with ExitStack() as ctx:
        def sem(name):
            return ctx.enter_context(nc.semaphore(name))

        def sb(name, shape, dt=F32, scope=ctx):
            return scope.enter_context(nc.sbuf_tensor(name, shape, dt))

        ps = ctx.enter_context(nc.psum_tensor("ps", [P, 8, 512], F32))

        x = sb("x", [P, KC, N])
        convh = sb("convh", [P, NF * 2, 32])
        rb = sb("rb", [P, N])
        acc = sb("acc", [P, N])
        sq = sb("sq", [P, 2, PAD + N])
        ident = sb("ident", [P, P])
        ones = sb("ones", [P, P])
        cwT = sb("cwT", [P, DEPTH * 3 * 2 * NF])
        cbT = sb("cbT", [P, DEPTH * 2 * NF])
        gT = sb("gT", [P, 6 * KC])
        sel = sb("sel", [NS * HIST, 4, NS])
        invc = sb("invc", [P, 4, PAD])
        hsum = sb("hsum", [P, KC, NS])
        utail = sb("utail", [P, 2 * NF, CT])
        ctm = sb("ctm", [CT, 2, 512])
        rtok = sb("rtok", [P, 9])
        rtmp = sb("rtmp", [P, 4, 9])
        stage = sb("stage", [P, 3, 1024])

        r1 = ExitStack()
        xh = sb("xh", [P, KC, N], F32R, r1)
        xl = sb("xl", [P, KC, N], F32R, r1)
        r1.close()
        r1 = ExitStack()
        xin = sb("xin", [P, 8, D], F32, r1)
        xsin = sb("xsin", [NS, D], F32, r1)
        phist = sb("phist", [NS * HIST, D], F32, r1)
        chin = sb("chin", [32, 2 * F], F32, r1)
        vA = sb("vA", [88, 3, P], F32, r1)
        vB = sb("vB", [88, P], F32, r1)
        vC = sb("vC", [48, P], F32, r1)
        r1.close()
        r1 = ExitStack()
        qt = sb("qt", [P, 2, QW], F32, r1)
        kvt = sb("kvt", [P, 4, 2 * QW], F32, r1)
        qT = sb("qT", [P, 2, QW], F32, r1)
        kT = sb("kT", [P, 3, QW], F32, r1)
        prob = sb("prob", [P, 2, 1024], F32, r1)
        probT = sb("probT", [P, 2, 1024], F32, r1)
        osb = sb("osb", [P, 3, OW], F32, r1)
        maskf = sb("maskf", [P, 3, P], F32, r1)
        mask = sb("mask", [P, 3, QW], BF16, r1)
        identb = sb("identb", [P, P], BF16, r1)
        qn = sb("qn", [NS, GROUPS, QW], F32, r1)
        samp = sb("samp", [P, 84], F32, r1)
        r1.close()
        r1 = ExitStack()
        om = sb("om", [P, 4, GROUPS, OW], F32, r1)
        ow = sb("ow", [P, 2, 4, GROUPS * HEADS], F32, r1)
        ot = sb("ot", [P, 2, 2, QW], F32, r1)
        yst = sb("yst", [P, 2, 8, P], F32, r1)
        yss = sb("yss", [NS, D], F32, r1)
        r1.close()
        sb("region1", [P, 2 * KC, N], F32, ctx)

        r2 = ExitStack()
        wh = sb("wh", [P, 3, 1024], F32R, r2)
        wl = sb("wl", [P, 3, 1024], F32R, r2)
        ua = sb("ua", [P, 2 + N], F32, r2)
        ub = sb("ub", [P, 2 + N], F32, r2)
        ca = sb("ca", [P, N], F32, r2)
        cb = sb("cb", [P, N], F32, r2)
        gh = sb("gh", [P, 2, N], F32R, r2)
        gl = sb("gl", [P, 2, N], F32R, r2)
        r2.close()
        r2 = ExitStack()
        sb("over_w", [P, 6, 1024], F32, r2)
        xn = sb("xn", [P, KC, PAD + N], F32, r2)
        swin = sb("swin", [P, 2, PAD + N], F32, r2)
        r2.close()

        r2 = ExitStack()
        wp1h = sb("wp1h", [P, KC, HW], F32R, r2)
        wp1l = sb("wp1l", [P, KC, HW], F32R, r2)
        sb("over_w1", [P, 2048], F32, r2)
        wp0h = sb("wp0h", [P, KC, HW], F32R, r2)
        wp0l = sb("wp0l", [P, KC, HW], F32R, r2)
        sb("over_u", [P, 36], F32, r2)
        wp2h = sb("wp2h", [P, KC, HW], F32R, r2)
        wp2l = sb("wp2l", [P, KC, HW], F32R, r2)
        sb("over_g", [P, 32], F32, r2)
        kn = sb("kn", [P, 3, QW], F32, r2)
        rot = sb("rot", [P, 2, 9, 16], F32, r2)
        hg = sb("hg", [P, 2, HD], F32, r2)
        hs = sb("hs", [P, 5, HEADS], F32, r2)
        r2.close()
        wph, wpl = (wp0h, wp1h, wp2h), (wp0l, wp1l, wp2l)
        r2 = ExitStack()
        oTh = sb("oTh", [P, 4, N], F32R, r2)
        oTl = sb("oTl", [P, 4, N], F32R, r2)
        r2b = ExitStack()
        qb = sb("qb", [P, 2, GROUPS, QW], F32, r2b)
        kc = sb("kc", [P, 3, QW], F32, r2b)
        vc = sb("vc", [P, GROUPS, QW], F32, r2b)
        prod = sb("prod", [P, 1, QW], F32, r2b)
        r2b.close()
        woh = sb("woh", [P, 4, D], F32R, r2)
        wol = sb("wol", [P, 4, D], F32R, r2)
        r2.close()
        sq_flat = sq[:, :, :].rearrange("p s n -> p (s n)")
        sc = sq_flat[:, 0:192]
        sall = sq_flat[0:64, 192:192 + SK]
        pT = sq_flat[:, 520:520 + 3 * NS * 32]
        snew = sq_flat[0:NS, 1288:1312]
        bnew = sq_flat[0:NS, 1312:1504]
        stat = sq_flat[0:64, 1504:1508]
        an = sq_flat[0:64, 1508:1532]
        pnew = sq_flat[0:NS, 1532:1556]
        selS = samp[:, 0:4]
        sel8 = samp[0:64, 4:12]
        del8 = samp[0:64, 12:20]
        del64 = samp[0:NS, 20:84]
        diag = kc[:, 0, :]
        om1 = rb[:, 0:QW]
        om2 = acc[:, 0:QW]
        onew = rb[0:NS, QW:2 * QW]

        kvs = nc.dram_tensor("kvs", [GROUPS, N, 2, QW], F32, kind="Internal").ap()
        qs = nc.dram_tensor("qs", [GROUPS, N, QW], F32, kind="Internal").ap()
        os_ = nc.dram_tensor("os_", [GROUPS, T, OW], F32, kind="Internal").ap()

        in_id, in_ph, in_xs, in_v, in_ch = (sem(n) for n in ("in_id", "in_ph", "in_xs", "in_v", "in_ch"))
        in_x = [sem(f"in_x{i}") for i in range(4)]
        set0 = sem("set0")
        pro_pe = sem("pro_pe")
        pro_v = sem("pro_v")
        pro_a = sem("pro_a")
        vec = sem("vec")
        ssq = sem("ssq")
        rn = sem("rn")
        rn_a = sem("rn_a")
        dg = sem("dg")
        rb_pe = sem("rb_pe")
        rb_v = sem("rb_v")
        wp_in, wp_h, wp_l = sem("wp_in"), sem("wp_h"), sem("wp_l")
        xn_v = sem("xn_v")
        tl_pe, tl_a = sem("tl_pe"), sem("tl_a")
        win_v, win_p = sem("win_v"), sem("win_p")
        dif = sem("dif")
        dif_h, dif_l = sem("dif_h"), sem("dif_l")
        pool_pe, pool_x = sem("pool_pe"), sem("pool_x")
        out_w = sem("out_w")
        tl_out = sem("tl_out")

        split_sq, split_acc = sem("split_sq"), sem("split_acc")
        split_hi, split_lo = sem("split_hi"), sem("split_lo")

        class Split:
            def __init__(self, n):
                self.sq = self.hi = self.lo = KC * n
                self.acc = (KC - 1) * n

        ffn_stage = [sem(f"ffn_stage{i}") for i in range(3)]
        ct_out = [sem(f"ct_out{i}") for i in range(2)]

        class Ffn:
            def __init__(self, L):
                n = f"f{L}_"
                self.stage = 16 * SLABS // 3 * L
                self.ct_out = [32 * 6 * L, 32 * 5 * L]
                self.hi = sem(n + "hi")
                self.lo = sem(n + "lo")
                self.up = sem(n + "up")
                self.down = sem(n + "down")
                self.A = sem(n + "A")
                self.B = sem(n + "B")
                self.r = sem(n + "r")
                self.ra = sem(n + "ra")
                self.ut = sem(n + "ut")
                self.tap = sem(n + "tap")
                self.conv = sem(n + "conv")
                self.silu = sem(n + "silu")
                self.prod = sem(n + "prod")
                self.gh = sem(n + "gh")
                self.gl = sem(n + "gl")
                self.ct_pe = sem(n + "ct_pe")
                self.ct = sem(n + "ct")

        split = [Split(0), Split(1), Split(2)]
        ffn = [Ffn(0), Ffn(1)]
        piece_in = [sem(f"piece_in{i}") for i in range(3)]
        pj_h, pj_l = sem("pj_h"), sem("pj_l")
        pj_pe = sem("pj_pe")
        pj_n = sem("pj_n")
        pj_half = sem("pj_half")
        pj_a = sem("pj_a")
        pj_sq, pj_rt = sem("pj_sq"), sem("pj_rt")
        pj_s = sem("pj_s")
        pj_v = sem("pj_v")
        pj_r = sem("pj_r")
        rows_out = [sem(f"rows_out{i}") for i in range(3)]
        kv_out = sem("kv_out")
        at_q = [sem(f"at_q{i}") for i in range(2)]
        at_kv = [sem(f"at_kv{i}") for i in range(4)]
        at_tp, at_tc = sem("at_tp"), sem("at_tc")
        at_mk = sem("at_mk")
        at_s = sem("at_s")
        at_m = sem("at_m")
        at_e = sem("at_e")
        at_pt = sem("at_pt")
        at_pa, at_pb = sem("at_pa"), sem("at_pb")
        at_o, at_oc = sem("at_o"), sem("at_oc")
        in_mask, in_new, in_diag = sem("in_mask"), sem("in_new"), sem("in_diag")
        sm_q = [sem(f"sm_q{i}") for i in range(2)]
        sm_k = [sem(f"sm_k{i}") for i in range(3)]
        sm_vin = [sem(f"sm_vin{i}") for i in range(3)]
        sm_z = sem("sm_z")
        sm_p, sm_r = sem("sm_p"), sem("sm_r")
        sm_new = sem("sm_new")
        sm_pe = sem("sm_pe")
        sm_e = sem("sm_e")
        sm_st = sem("sm_st")
        sm_o = sem("sm_o")
        sm_f, sm_fh, sm_fl = sem("sm_f"), sem("sm_fh"), sem("sm_fl")
        mg_in = [sem(f"mg_in{i}") for i in range(4)]
        mg_a, mg_e, mg_v, mg_p = sem("mg_a"), sem("mg_e"), sem("mg_v"), sem("mg_p")
        mg_pe, mg_h, mg_l = sem("mg_pe"), sem("mg_h"), sem("mg_l")
        wo_h, wo_l, wo_pe, wo_x = sem("wo_h"), sem("wo_l"), sem("wo_pe"), sem("wo_x")
        y_pe, y_a, y_v, y_s, ys_out = sem("y_pe"), sem("y_a"), sem("y_v"), sem("y_s"), sem("ys_out")
        block = ctx.enter_context(nc.Block())

        def wait(e, s, v):
            if not isinstance(v, int) or v > 0:
                e.wait_ge(s, v)

        def bank3(s):
            return ps[:, 3 * s:3 * s + 3, 0:NW]

        def cols3(t):
            return t.rearrange("p (c n) -> p c n", c=NC)

        def group(pe, bank0, parts, pre=None):
            for i, (w, m) in enumerate(parts):
                if pre:
                    pre(i)
                for c in range(NC):
                    mm = pe.matmul(ps[:, bank0 + c, 0:NW], w, m[:, c * NW:(c + 1) * NW],
                                   start=(i == 0), stop=(i == len(parts) - 1))
            return mm

        def three(w_hi, w_lo, m_hi, m_lo):
            return [(w_hi, m_hi), (w_hi, m_lo), (w_lo, m_hi)]

        def act_split(act, S, d, gain):
            if d >= 3:
                act.wait_ge(split_acc, S.acc + d - 2)
            nc.scalar.activation(acc[:, :] if d == 0 else sq[:, d % 2, 0:N], x[:, d, :], ACT.Square).then_inc(split_sq, 1)
            if gain is None:
                nc.scalar.activation(xh[:, d, :], x[:, d, :], ACT.Copy).then_inc(split_hi, 1)
            else:
                nc.scalar.activation(xh[:, d, :], x[:, d, :], ACT.Copy,
                                     scale=gT[:, gain + d:gain + d + 1]).then_inc(split_hi, 1)

        def dve_split(v, S, d, gain):
            v.wait_ge(split_hi, S.hi + d + 1)
            if gain is None:
                nc.vector.tensor_tensor(xl[:, d, :], x[:, d, :], xh[:, d, :].bitcast(F32), ALU.subtract).then_inc(split_lo, 1)
            else:
                nc.vector.scalar_tensor_tensor(out=xl[:, d, :], in0=x[:, d, :], scalar=gT[:, gain + d:gain + d + 1],
                                               in1=xh[:, d, :].bitcast(F32), op0=ALU.mult,
                                               op1=ALU.subtract).then_inc(split_lo, 1)

        def pool_split(g, S):
            for d in range(1, KC):
                g.wait_ge(split_sq, S.sq + d + 1)
                if d >= 2:
                    g.wait_ge(split_acc, S.acc + d - 1)
                nc.gpsimd.tensor_tensor(acc[:, :], acc[:, :], sq[:, d % 2, 0:N], ALU.add).then_inc(split_acc, 1)

        CH = 16

        def sp_start(sp):
            sp.dma_start(ident[:, :], a["ident"]).then_inc(in_id, 16)
            for i in range(4):
                sp.dma_start(xin[:, 2 * i:2 * i + 2, :], a["x_prompt"][0, 2 * i * P:(2 * i + 2) * P, :].rearrange(
                    "(t p) d -> p t d", p=P)).then_inc(in_x[i], 16)
            sp.dma_start(xsin[:, :], a["x_sample"].rearrange("s o d -> (s o) d")).then_inc(in_xs, 16)
            for g0, n, src in ((G_POOL, KC, a["g_pool"]), (G_SCALE, KC, a["pool_scale"]), (G_FFN, 2 * KC, a["g_ffn"]),
                               (G_ATTN, KC, a["g_attn"])):
                sp.dma_start(vC[g0:g0 + n, :], src.rearrange("l (c p) -> (l c) p", p=P)).then_inc(in_v, 16)
            sp.dma_start(vC[G_KV:G_KV + KC, :], a["g_kv"].rearrange("(c p) -> c p", p=P)).then_inc(in_v, 16)
            sp.dma_start(vB[:, :], a["conv_b"].rearrange("l (c p) -> (l c) p", p=P)).then_inc(in_v, 16)
            sp.dma_start(vA[:, :, :], a["conv_w"].rearrange("l j (c p) -> (l j c) p", p=P).rearrange(
                "(b q) p -> q b p", q=88)).then_inc(in_v, 16)
            sp.dma_start(sel[:, :, :], a["sel"]).then_inc(in_ph, 16)
            sp.dma_start(invc[:, :, :], a["invc"]).then_inc(in_ph, 16)
            sp.dma_start(phist[:, :], a["state_pool"][0].rearrange("s h d -> (s h) d")).then_inc(in_ph, 16)
            sp.dma_start(stage[:, 1:3, :].rearrange("p s n -> p (s n)").rearrange("p (q e) -> p q e", e=256),
                         a["w_pool"][0].rearrange("g (k p) e -> p (g k) e", p=P)).then_inc(wp_in, 16)
            sp.dma_start(chin[:, :], a["state_conv"].rearrange("l s j f -> (l s j) f")).then_inc(in_ch, 16)
            sp.dma_start(o["pool_sample"][0, :, 0:HIST - 1, :], a["state_pool"][0, :, 1:HIST, :]).then_inc(out_w, 16)
            for L in range(DEPTH):
                sp.dma_start(o["conv_sample"][L, :, 0, :], a["state_conv"][L, :, 1, :]).then_inc(out_w, 16)

        def sp_pool_tails(sp):
            sp.wait_ge(tl_a, 2)
            sp.dma_start(o["pool_prompt"][0, 0], acc[0:HIST, 0:D]).then_inc(tl_out, 16)
            sp.dma_start(o["pool_sample"][0, :, HIST - 1, :], acc[HIST:TAIL, 0:D]).then_inc(tl_out, 16)

        def pe_start(pe):
            pe.wait_ge(in_id, 16)
            for g in range(22):
                b = g % 8
                if g >= 8:
                    pe.wait_ge(pro_v if g % 2 == 0 else pro_a, (g - 8) // 2 + 1)
                if g < 16:
                    pe.wait_ge(in_x[g // 4], 16)
                    for i in range(4):
                        d = 4 * (g % 2) + i
                        mm = pe.transpose(ps[:, b, i * P:(i + 1) * P], xin[:, g // 2, d * P:(d + 1) * P], ident[:, :])
                elif g == 16:
                    pe.wait_ge(in_xs, 16)
                    for d in range(KC):
                        mm = pe.transpose(ps[:, b, d * NS:(d + 1) * NS], xsin[:, d * P:(d + 1) * P], ident[0:NS, 0:NS])
                elif g == 17:
                    pe.wait_ge(in_v, 16 * 7)
                    pe.transpose(ps[:, b, 0:48], vC[:, :], ident[0:48, 0:48])
                    pe.transpose(ps[:, b, 48:136], vB[:, :], ident[0:88, 0:88])
                    for i in range(3):
                        mm = pe.transpose(ps[:, b, 136 + 88 * i:224 + 88 * i], vA[:, i, :], ident[0:88, 0:88])
                elif g == 18:
                    pe.wait_ge(in_ph, 16 * 3)
                    for d in range(KC):
                        mm = pe.matmul(ps[:, b, d * NS:(d + 1) * NS], phist[:, d * P:(d + 1) * P], sel[:, d // 2, :],
                                       start=True, stop=True)
                else:
                    if g == 19:
                        pe.wait_ge(pro_v, 8)
                        pe.wait_ge(pro_a, 8)
                        pe.wait_ge(dg, 9)
                        pe.wait_ge(set0, 2)
                        for c in range(NC):
                            mm = pe.matmul(ps[:, 5 + c, 0:NW], ones[:, :], acc[:, c * NW:(c + 1) * NW],
                                           start=True, stop=True)
                        mm.then_inc(rb_pe, 1)
                        pe.wait_ge(in_ch, 16)
                    if g == 21:
                        pe.wait_ge(rb_v, 1)
                    for i in range(CH * (g - 19), min(CH * (g - 18), 2 * NF)):
                        c = i - CH * (g - 19)
                        mm = pe.transpose(ps[:, b, 32 * c:32 * c + 32], chin[:, i * P:(i + 1) * P], ident[0:32, 0:32])
                mm.then_inc(pro_pe, 1)

        def pro_copy(g):
            b = g % 8
            if g < 16:
                return [(x[:, 4 * (g % 2):4 * (g % 2) + 4, (g // 2) * P:(g // 2 + 1) * P],
                         ps[:, b, :].rearrange("p (i n) -> p i n", i=4))]
            if g == 16:
                return [(x[:, :, T:N], ps[:, b, 0:KC * NS].rearrange("p (i n) -> p i n", i=KC))]
            if g == 17:
                return [(gT[:, :], ps[:, b, 0:48]), (cbT[:, :], ps[:, b, 48:136]), (cwT[:, :], ps[:, b, 136:400])]
            if g == 18:
                return [(hsum[:, :, :], ps[:, b, 0:KC * NS].rearrange("p (i n) -> p i n", i=KC))]
            i0, i1 = CH * (g - 19), min(CH * (g - 18), 2 * NF)
            return [(convh[:, i0:i1, :], ps[:, b, 0:32 * (i1 - i0)].rearrange("p (i n) -> p i n", n=32))]

        def newton(v, m, y, t, s, n, s_a, n_a):
            v.wait_ge(s_a, n_a)
            nc.vector.reciprocal(y, y).then_inc(s, 1)
            v.wait_ge(s, n + 1)
            nc.vector.tensor_tensor(t, y, y, ALU.mult).then_inc(s, 1)
            v.wait_ge(s, n + 2)
            nc.vector.scalar_tensor_tensor(out=t, in0=t, scalar=-0.5, in1=m, op0=ALU.mult, op1=ALU.mult).then_inc(s, 1)
            v.wait_ge(s, n + 3)
            nc.vector.scalar_tensor_tensor(out=y, in0=t, scalar=1.5, in1=y, op0=ALU.add, op1=ALU.mult).then_inc(s, 1)
            v.wait_ge(s, n + 4)

        def dve_windows(v, c, buf, s, n, add):
            cur = xn[:, c, :]
            k, i = 1, 0
            first = (n % 2)
            while k < WINDOWS[c // 2]:
                dst = buf[:, (first + i) % 2, :]
                if i:
                    v.wait_ge(s, n + i)
                lo = 2 * k - 1
                add(dst[:, lo:PAD + T], cur[:, lo:PAD + T], cur[:, lo - k:PAD + T - k]).then_inc(s, 1)
                cur, k, i = dst, 2 * k, i + 1
            return cur, n + i

        def window_plan(par):
            plan, n = {}, 0
            for g in range(4):
                steps = g + 1
                plan[2 * g + par] = (n, (n + steps - 1) % 2, n + steps)
                n += steps
            return plan
        PLAN = {**window_plan(0), **window_plan(1)}

        def dve_start(v):
            for g in range(0, 16, 2):
                v.wait_ge(pro_pe, g + 1)
                for dst, src in pro_copy(g):
                    nc.vector.tensor_copy(dst, src).then_inc(pro_v, 1)
            v.wait_ge(pro_pe, 17)
            for dst, src in pro_copy(16):
                nc.vector.tensor_copy(dst, src).then_inc(pro_v, 1)
            m, y, t = rtmp[:, 0, :], rtok[:, :], rtmp[:, 2, :]
            v.wait_ge(ssq, 9)
            nc.vector.tensor_scalar(m, rtmp[:, 3, :], 1.0 / D, EPS, ALU.mult, ALU.add).then_inc(rn, 1)
            newton(v, m, y, t, rn, 1, rn_a, 1)
            v.wait_ge(in_id, 16)
            for i in range(8):
                nc.vector.tensor_scalar(acc[:, i * P:(i + 1) * P], ident[:, :], rtok[:, i:i + 1], None,
                                        ALU.mult).then_inc(dg, 1)
            nc.vector.tensor_scalar(acc[:, T:N], ident[:, 0:NS], rtok[:, 8:9], None, ALU.mult).then_inc(dg, 1)
            v.wait_ge(pro_pe, 19)
            for dst, src in pro_copy(18):
                nc.vector.tensor_copy(dst, src).then_inc(pro_v, 1)
            v.wait_ge(rb_pe, 1)
            nc.vector.tensor_copy(cols3(rb[:, :]), ps[:, 5:8, 0:NW]).then_inc(rb_v, 1)
            v.wait_ge(rb_v, 1)
            v.wait_ge(vec, 3)
            v.wait_ge(pro_a, 8)
            v.wait_ge(pro_v, 9)
            for c in range(KC):
                nc.vector.scalar_tensor_tensor(out=xn[:, c, PAD:], in0=x[:, c, :], scalar=gT[:, G_POOL + c:G_POOL + c + 1],
                                               in1=rb[:, :], op0=ALU.mult, op1=ALU.mult).then_inc(xn_v, 1)
            v.wait_ge(pro_pe, 21)
            for dst, src in pro_copy(20):
                nc.vector.tensor_copy(dst, src).then_inc(pro_v, 1)
            v.wait_ge(set0, 2)
            v.wait_ge(xn_v, KC)
            v.wait_ge(wp_h, 1)
            nc.vector.tensor_tensor(wl[:, 1:3, :], stage[:, 1:3, :], wh[:, 1:3, :].bitcast(F32), ALU.subtract).then_inc(wp_l, 1)
            dve_ffn_slab0(v, ffn[0])

            def difference(c, i):
                w, par = WINDOWS[c // 2], c % 2
                n, last, done = PLAN[c]
                s = (sq if par else swin)[:, last, :]
                v.wait_ge(win_p if par else win_v, done)
                nc.vector.tensor_tensor(s[:, PAD:2 * PAD], s[:, PAD:2 * PAD], invc[:, c // 2, :], ALU.mult).then_inc(dif, 1)
                nc.vector.tensor_tensor(s[:, PAD + T:], hsum[:, c, :], xn[:, c, PAD + T:], ALU.add).then_inc(dif, 1)
                nc.vector.scalar_tensor_tensor(out=s[:, 2 * PAD:PAD + T], in0=s[:, 2 * PAD:PAD + T], scalar=1.0 / w,
                                               in1=xn[:, c, 2 * PAD:PAD + T], op0=ALU.mult,
                                               op1=ALU.subtract).then_inc(dif, 1)
                v.wait_ge(dif, 5 * i + 1)
                nc.vector.tensor_tensor(s[:, PAD:2 * PAD], s[:, PAD:2 * PAD], xn[:, c, PAD:2 * PAD],
                                        ALU.subtract).then_inc(dif, 1)
                v.wait_ge(dif, 5 * i + 2)
                nc.vector.scalar_tensor_tensor(out=s[:, PAD + T:], in0=s[:, PAD + T:], scalar=1.0 / w,
                                               in1=xn[:, c, PAD + T:], op0=ALU.mult, op1=ALU.subtract).then_inc(dif, 1)

            def tail(c, i):
                last = PLAN[c][1]
                v.wait_ge(dif_h, i + 1)
                nc.vector.tensor_tensor(xl[:, c, :], (sq if c % 2 else swin)[:, last, PAD:], xh[:, c, :].bitcast(F32),
                                        ALU.subtract).then_inc(dif_l, 1)

            v.wait_ge(pro_v, 11)
            for g in range(4):
                if g:
                    v.wait_ge(dif_l, 2 * g)
                    v.wait_ge(dif_h, 2 * g)
                dve_windows(v, 2 * g, swin, win_v, PLAN[2 * g][0],
                            lambda d, p, q: nc.vector.tensor_tensor(d, p, q, ALU.add))
                difference(2 * g, 2 * g)
                difference(2 * g + 1, 2 * g + 1)
                tail(2 * g, 2 * g)
                tail(2 * g + 1, 2 * g + 1)
            for d in range(KC):
                v.wait_ge(pool_pe, d + 1)
                nc.vector.scalar_tensor_tensor(out=cols3(x[:, d, :]), in0=bank3(d % 2), scalar=gT[:, G_SCALE + d:G_SCALE + d + 1],
                                               in1=cols3(x[:, d, :]), op0=ALU.mult, op1=ALU.add).then_inc(pool_x, 1)
                if d % 2 == 1:
                    dve_split(v, split[0], d - 1, G_FFN)
                    dve_split(v, split[0], d, G_FFN)

        def pool_start(g):
            nc.gpsimd.memset(xn[:, :, 0:PAD], 0.0).then_inc(set0, 1)
            nc.gpsimd.memset(ones[:, :], 1.0).then_inc(set0, 1)
            nc.gpsimd.memset(rtmp[:, 3, :], 1.0).then_inc(set0, 1)
            g.wait_ge(xn_v, KC)
            for i in range(4):
                if i:
                    g.wait_ge(dif_l, 2 * i)
                dve_windows(g, 2 * i + 1, sq, win_p, PLAN[2 * i + 1][0],
                            lambda d, p, q: nc.gpsimd.tensor_tensor(d, p, q, ALU.add))
            pool_split(g, split[0])

        def act_start(act):
            act.wait_ge(set0, 3)
            for t in range(8):
                act.wait_ge(in_x[t // 2], 16)
                wait(act, ssq, t)
                nc.scalar.activation(sq[:, 0, 0:D], xin[:, t, :], ACT.Square, accum_out=rtmp[:, 3, t:t + 1]).then_inc(ssq, 1)
                act.wait_ge(pro_pe, 2 * t + 2)
                for dst, src in pro_copy(2 * t + 1):
                    nc.scalar.activation(dst, src, ACT.Copy).then_inc(pro_a, 1)
            act.wait_ge(in_xs, 16)
            act.wait_ge(ssq, 8)
            nc.scalar.activation(sq[0:NS, 0, 0:D], xsin[:, :], ACT.Square, accum_out=rtmp[0:NS, 3, 8:9]).then_inc(ssq, 1)
            act.wait_ge(rn, 1)
            nc.scalar.activation(rtok[:, :], rtmp[:, 0, :], ACT.Sqrt).then_inc(rn_a, 1)
            act.wait_ge(pro_pe, 18)
            for dst, src in pro_copy(17):
                nc.scalar.activation(dst, src, ACT.Copy).then_inc(vec, 1)
            act.wait_ge(wp_in, 16)
            nc.scalar.activation(wh[:, 1:3, :], stage[:, 1:3, :], ACT.Copy).then_inc(wp_h, 1)
            act_ffn_slab0(act, ffn[0], [])
            for g in (19, 21):
                act.wait_ge(pro_pe, g + 1)
                for dst, src in pro_copy(g):
                    nc.scalar.activation(dst, src, ACT.Copy).then_inc(pro_a, 1)
            for h in range(2):
                act.wait_ge(tl_pe, h + 1)
                nc.scalar.activation(acc[0:TAIL, h * 512:(h + 1) * 512], ps[0:TAIL, 6 + h, :], ACT.Copy).then_inc(tl_a, 1)
            for c in range(KC):
                act.wait_ge(dif, 5 * c + 5)
                nc.scalar.activation(xh[:, c, :], (sq if c % 2 else swin)[:, PLAN[c][1], PAD:], ACT.Copy).then_inc(dif_h, 1)
            act.wait_ge(tl_out, 32)
            act.wait_ge(dif_l, KC)
            for d in range(KC):
                act.wait_ge(pool_x, d + 1)
                act.wait_ge(pool_pe, 2 * (d // 2) + 2)
                act_split(act, split[0], d, G_FFN)

        def pe_pool(pe):
            pe.wait_ge(xn_v, KC)
            pe.wait_ge(rb_v, 1)
            for h in range(2):
                for i in range(4):
                    mm = pe.transpose(ps[0:TAIL, 6 + h, i * P:(i + 1) * P], xn[:, 4 * h + i, PAD + N - TAIL:], ident[:, :])
                mm.then_inc(tl_pe, 1)
            pe.wait_ge(wp_l, 1)
            pe.wait_ge(pro_v, 11)
            pe.wait_ge(pro_a, 10)
            pw, pwt = (t[:, 1:3, :].rearrange("p s n -> p (s n)") for t in (wh, wl))
            for g in range(4):
                pe.wait_ge(dif_l, 2 * g + 2)
                for e in range(2):
                    if g:
                        pe.wait_ge(pool_x, 2 * g + e - 1)
                    parts = []
                    for k in range(2):
                        at = (2 * g + k) * 256 + e * P
                        parts += three(pw[:, at:at + P], pwt[:, at:at + P], xh[:, 2 * g + k, :], xl[:, 2 * g + k, :])
                    group(pe, 3 * e, parts).then_inc(pool_pe, 1)


        def slot_of(k):
            return (2 + k) % 3

        def up_src(L, half, f):
            w = a["w_up"][L].rearrange("(k p) n -> p k n", p=P)
            return w[:, :, bass.ds(f * P + half * F, P)]

        def down_src(L, f):
            return a["w_down"][L][bass.ds(f * P, P), :]

        def sp_ffn(sp, L, S, begin):
            def load(n, slot, src, up):
                if isinstance(n, int) and n < 3:
                    begin(sp, n)
                else:
                    sp.wait_ge(S.hi, n - 2)
                    sp.wait_ge(S.lo, n - 2)
                dst = stage[:, slot, :]
                if up:
                    dst = dst.rearrange("p (k n) -> p k n", k=KC)
                sp.dma_start(dst, src).then_inc(ffn_stage[slot], 16)

            load(0, 0, up_src(L, 0, 0), True)
            load(1, 1, up_src(L, 1, 0), True)
            load(2, 2, up_src(L, 0, 1), True)

            def rest(j, last):
                n0 = 6 * j + 2
                load(n0 + 1, slot_of(1), up_src(L, 1, 2 * j + 1), True)
                if last:
                    load(n0 + 2, slot_of(2), down_src(L, 2 * j), False)
                    load(n0 + 3, slot_of(3), down_src(L, 2 * j + 1), False)
                    return
                load(n0 + 2, slot_of(2), up_src(L, 0, 2 * j + 2), True)
                load(n0 + 3, slot_of(3), up_src(L, 1, 2 * j + 2), True)
                load(n0 + 4, slot_of(4), down_src(L, 2 * j), False)
                load(n0 + 5, slot_of(5), down_src(L, 2 * j + 1), False)
                load(n0 + 6, slot_of(6), up_src(L, 0, 2 * j + 3), True)

            with sp.Fori(0, LAST) as j:
                rest(j, False)
            rest(LAST, True)

        def act_slab(act, S, j, k, free):
            act.wait_ge(ffn_stage[slot_of(k)], 32 * j + (S.stage + 16 * ((2 + k) // 3 + 1)))
            for s, v in free:
                wait(act, s, v)
            nc.scalar.activation(wh[:, slot_of(k), :], stage[:, slot_of(k), :], ACT.Copy).then_inc(S.hi, 1)

        def dve_slab(v, S, j, k):
            v.wait_ge(S.hi, 6 * j + 3 + k)
            nc.vector.tensor_tensor(wl[:, slot_of(k), :], stage[:, slot_of(k), :], wh[:, slot_of(k), :].bitcast(F32),
                                    ALU.subtract).then_inc(S.lo, 1)

        def pe_up(pe, S, slot, slab, sset, free, Sx=None):
            pe.wait_ge(S.lo, slab + 1)
            if free is not None:
                pe.wait_ge(*free)
            parts = []
            for k in range(KC):
                w, wt = wh[:, slot, k * P:(k + 1) * P], wl[:, slot, k * P:(k + 1) * P]
                parts += three(w, wt, xh[:, k, :], xl[:, k, :])

            def pre(i):
                if Sx is not None and i % 3 == 0:
                    pe.wait_ge(split_lo, Sx.lo + i // 3 + 1)
            group(pe, 3 * sset, parts, pre).then_inc(S.up, 1)

        def pe_down(pe, S, j, slots, slabs, baseA, baseB, after=None):
            pe.wait_ge(S.lo, slabs)
            pe.wait_ge(S.gl, 2 * j + 2)
            for d in range(KC):
                pe.wait_ge(*((S.A, baseA + d // 2) if d % 2 == 0 else (S.B, baseB + d // 2)))
                parts = []
                for c in range(2):
                    w = wh[:, slots[c], d * P:(d + 1) * P]
                    wt = wl[:, slots[c], d * P:(d + 1) * P]
                    parts += three(w, wt, gh[:, c, :], gl[:, c, :])
                group(pe, 3 * (d % 2), parts).then_inc(S.down, 1)
                if after is not None:
                    after(d)

        def pe_ffn(pe, L, S, Sx, freeA, after=None):
            pe_up(pe, S, 0, 0, 0, freeA, Sx)
            pe.wait_ge(split_acc, Sx.acc + KC - 1)
            for c in range(NC):
                mm = pe.matmul(ps[:, 3 + c, 0:NW], ones[:, :], acc[:, c * NW:(c + 1) * NW], start=True, stop=True)
            mm.then_inc(S.down, 1)
            pe_up(pe, S, 1, 1, 1, (S.B, 1))

            def ups(j):
                pe_up(pe, S, slot_of(0), 6 * j + 2, 0, (S.A, 6 * j + 1))
                pe_up(pe, S, slot_of(1), 6 * j + 3, 1, (S.B, 6 * j + 2))

            with pe.Fori(0, LAST) as j:
                ups(j)
                pe_up(pe, S, slot_of(2), 6 * j + 4, 0, (S.A, 6 * j + 2))
                pe_up(pe, S, slot_of(3), 6 * j + 5, 1, (S.B, 6 * j + 3))
                pe_down(pe, S, j, (slot_of(4), slot_of(5)), 6 * j + 8, 6 * j + 3, 6 * j + 4)
            j = LAST
            ups(j)
            pe_conv_tails(pe, S, (0, 1))

            def between(d):
                pe_conv_tails(pe, S, tails_after(d))
                if after is not None:
                    after(d)
            pe_down(pe, S, j, (slot_of(2), slot_of(3)), 6 * j + 6, 6 * j + 2, 6 * j + 3, between)

        def tails_after(d):
            return [q for q in (2 * d + 2, 2 * d + 3) if q < NF // 2]

        def pe_conv_tails(pe, S, some):
            pe.wait_ge(S.ut, 2 * NF)
            for q in some:
                if q >= 2:
                    pe.wait_ge(S.ct, q - 1)
                for i in range(4):
                    mm = pe.transpose(ps[0:CT, 6 + q % 2, i * P:(i + 1) * P], utail[:, 4 * q + i, :], ident[:, :])
                mm.then_inc(S.ct_pe, 1)

        def evac(v, S, u, up, sset, free):
            v.wait_ge(S.up, up)
            nc.vector.tensor_tensor(cols3(u[:, 2:2 + N]), bank3(sset), cols3(rb[:, :]), ALU.mult).then_inc(free, 1)

        def keep_tail(v, S, u, half, f, free, n):
            v.wait_ge(free, n)
            nc.vector.tensor_copy(utail[:, bass.ds(half * NF + f, 1), :].rearrange("p o c -> p (o c)"),
                                  u[:, T:2 + N]).then_inc(S.ut, 1)

        def conv_steps(v, L, S, f):
            def tap(c, u, half, t, own):
                w = cwT[:, bass.ds(f + (L * 3 + t) * 2 * NF + half * NF, 1)]
                if t == 1:
                    v.wait_ge(S.tap, 2 * f + 1 + half)
                else:
                    v.wait_ge(S.conv, 8 * f + own)
                nc.vector.scalar_tensor_tensor(out=c[:, 0:T], in0=u[:, t:t + T], scalar=w, in1=c[:, 0:T],
                                               op0=ALU.mult, op1=ALU.add).then_inc(S.conv, 1)
                if t == 0:
                    v.wait_ge(S.conv, 8 * f + own + 1)
                h = convh[:, bass.ds(f + half * NF, 1), L * 2 * NS + t:(L + 1) * 2 * NS:2].rearrange("p o s -> p (o s)")
                nc.vector.scalar_tensor_tensor(out=c[:, T:N], in0=h, scalar=w, in1=c[:, T:N],
                                               op0=ALU.mult, op1=ALU.add).then_inc(S.conv, 1)

            def prod():
                v.wait_ge(S.silu, f + 1)
                v.wait_ge(S.conv, 8 * f + 8)
                nc.vector.tensor_tensor(cb[:, :], ca[:, :], cb[:, :], ALU.mult).then_inc(S.prod, 1)
            return [lambda: tap(ca, ua, 0, 1, 0), lambda: tap(cb, ub, 1, 1, 0),
                    lambda: tap(ca, ua, 0, 0, 1), lambda: tap(cb, ub, 1, 0, 3), prod]

        def dve_gl(v, S, f, c):
            v.wait_ge(S.gh, f + 1)
            nc.vector.tensor_tensor(gl[:, c, :], cb[:, :], gh[:, c, :].bitcast(F32), ALU.subtract).then_inc(S.gl, 1)

        def add_x(v, S, d, down):
            v.wait_ge(S.down, down)
            nc.vector.tensor_tensor(cols3(x[:, d, :]), cols3(x[:, d, :]), bank3(d % 2),
                                    ALU.add).then_inc(S.A if d % 2 == 0 else S.B, 1)

        def dve_ffn_slab0(v, S):
            dve_slab(v, S, 0, -2)

        def dve_ffn(v, L, S, finish, meanwhile=None):
            dve_slab(v, S, 0, -1)
            dve_slab(v, S, 0, 0)
            m, y = sq[:, 0, 0:N], sq[:, 1, 0:N]
            v.wait_ge(S.down, 1)
            nc.vector.tensor_scalar(cols3(m), bank3(1), 1.0 / D, EPS, ALU.mult, ALU.add).then_inc(S.B, 1)
            v.wait_ge(S.ra, 1)
            nc.vector.reciprocal(rb[:, :], y).then_inc(S.r, 1)
            v.wait_ge(S.r, 1)
            nc.vector.tensor_tensor(y, rb[:, :], rb[:, :], ALU.mult).then_inc(S.r, 1)
            v.wait_ge(S.r, 2)
            nc.vector.scalar_tensor_tensor(out=m, in0=y, scalar=-0.5, in1=m, op0=ALU.mult, op1=ALU.mult).then_inc(S.r, 1)
            v.wait_ge(S.r, 3)
            nc.vector.scalar_tensor_tensor(out=rb[:, :], in0=m, scalar=1.5, in1=rb[:, :], op0=ALU.add,
                                           op1=ALU.mult).then_inc(S.r, 1)
            v.wait_ge(S.r, 4)
            nc.vector.memset(ua[:, 0:2], 0.0).then_inc(S.r, 1)
            nc.vector.memset(ub[:, 0:2], 0.0).then_inc(S.r, 1)
            v.wait_ge(S.r, 6)
            evac(v, S, ua, 1, 0, S.A)
            keep_tail(v, S, ua, 0, 0, S.A, 1)
            evac(v, S, ub, 2, 1, S.B)
            keep_tail(v, S, ub, 1, 0, S.B, 2)
            for step in conv_steps(v, L, S, 0):
                step()

            def body(j, last):
                dve_slab(v, S, j, 1)
                dve_slab(v, S, j, 2)
                dve_gl(v, S, 2 * j, 0)
                evac(v, S, ua, 4 * j + 3, 0, S.A)
                dve_slab(v, S, j, 3)
                keep_tail(v, S, ua, 0, 2 * j + 1, S.A, 6 * j + 2)
                evac(v, S, ub, 4 * j + 4, 1, S.B)
                if not last:
                    dve_slab(v, S, j, 4)
                keep_tail(v, S, ub, 1, 2 * j + 1, S.B, 6 * j + 3)
                for step in conv_steps(v, L, S, 2 * j + 1):
                    step()
                dve_gl(v, S, 2 * j + 1, 1)
                if last:
                    return
                evac(v, S, ua, 4 * j + 5, 0, S.A)
                dve_slab(v, S, j, 5)
                keep_tail(v, S, ua, 0, 2 * j + 2, S.A, 6 * j + 3)
                evac(v, S, ub, 4 * j + 6, 1, S.B)
                dve_slab(v, S, j, 6)
                keep_tail(v, S, ub, 1, 2 * j + 2, S.B, 6 * j + 4)
                steps = conv_steps(v, L, S, 2 * j + 2)
                for d in range(KC):
                    add_x(v, S, d, 8 * j + d + 2)
                    if d < len(steps):
                        steps[d]()

            with v.Fori(0, LAST) as j:
                body(j, False)
            body(LAST, True)
            if meanwhile is not None:
                meanwhile()
            for d in range(KC):
                add_x(v, S, d, 8 * LAST + d + 2)
                finish(v, d)

        def act_tap(act, L, S, f, c, u, half, free, n):
            act.wait_ge(free, n)
            wait(act, S.gl, f)
            nc.scalar.activation(c[:, :], u[:, 2:2 + N], ACT.Identity,
                                 bias=cbT[:, bass.ds(f + L * 2 * NF + half * NF, 1)],
                                 scale=cwT[:, bass.ds(f + (L * 3 + 2) * 2 * NF + half * NF, 1)]).then_inc(S.tap, 1)

        def act_silu(act, S, f):
            act.wait_ge(S.conv, 8 * f + 6)
            nc.scalar.activation(ca[:, :], ca[:, :], ACT.Silu).then_inc(S.silu, 1)

        def act_gh(act, S, f, c, down):
            act.wait_ge(S.prod, f + 1)
            wait(act, S.down, down)
            nc.scalar.activation(gh[:, c, :], cb[:, :], ACT.Copy).then_inc(S.gh, 1)

        def act_ffn_slab0(act, S, free):
            act_slab(act, S, 0, -2, free)

        def act_ffn(act, L, S, free12):
            act_slab(act, S, 0, -1, free12)
            act_slab(act, S, 0, 0, free12)
            act.wait_ge(S.B, 1)
            nc.scalar.activation(sq[:, 1, 0:N], sq[:, 0, 0:N], ACT.Sqrt).then_inc(S.ra, 1)
            act_tap(act, L, S, 0, ca, ua, 0, S.A, 1)
            act_tap(act, L, S, 0, cb, ub, 1, S.B, 2)
            act_silu(act, S, 0)

            def body(j, last):
                act_slab(act, S, j, 1, [(S.up, 4 * j + 1), (S.down, 8 * j + 1)])
                act_slab(act, S, j, 2, [(S.up, 4 * j + 2), (S.down, 8 * j + 1)])
                act_gh(act, S, 2 * j, 0, 8 * j + 1)
                act_slab(act, S, j, 3, [(S.up, 4 * j + 3)])
                act_tap(act, L, S, 2 * j + 1, ca, ua, 0, S.A, 6 * j + 2)
                if not last:
                    act_slab(act, S, j, 4, [(S.up, 4 * j + 4)])
                act_tap(act, L, S, 2 * j + 1, cb, ub, 1, S.B, 6 * j + 3)
                act_silu(act, S, 2 * j + 1)
                act_gh(act, S, 2 * j + 1, 1, 8 * j + 1)
                if last:
                    return
                act_slab(act, S, j, 5, [(S.up, 4 * j + 5)])
                act_tap(act, L, S, 2 * j + 2, ca, ua, 0, S.A, 6 * j + 3)
                act_slab(act, S, j, 6, [(S.up, 4 * j + 6)])
                act_tap(act, L, S, 2 * j + 2, cb, ub, 1, S.B, 6 * j + 4)
                act_silu(act, S, 2 * j + 2)

            with act.Fori(0, LAST) as j:
                body(j, False)
            body(LAST, True)

        def added(S, d):
            def ready(e):
                e.wait_ge(*((S.A, 6 * LAST + 3 + d // 2) if d % 2 == 0 else (S.B, 6 * LAST + 4 + d // 2)))
            return ready

        def act_conv_tails(act, L, S, some):
            for q in some:
                act.wait_ge(S.ct_pe, q + 1)
                if q >= 2 or L:
                    act.wait_ge(ct_out[q % 2], S.ct_out[q % 2] + 32 * (q // 2))
                nc.scalar.activation(ctm[:, q % 2, :], ps[0:CT, 6 + q % 2, :], ACT.Copy).then_inc(S.ct, 1)
                act.wait_ge(S.ct, q + 1)
                cols = slice(q * 512, (q + 1) * 512)
                act.dma_start(o["conv_prompt"][L, 0][:, cols], ctm[0:2, q % 2, :]).then_inc(ct_out[q % 2], 16)
                act.dma_start(o["conv_sample"][L, :, 1, cols], ctm[2:CT, q % 2, :]).then_inc(ct_out[q % 2], 16)

        MT = [P] * 8 + [NS]
        K0 = 5

        def pj_src(u, half, part, g, later):
            cols = slice(half * HW, (half + 1) * HW)
            if u == 2:
                w = a["w_q"][0].rearrange("(k p) (g n) -> g p k n", p=P, g=GROUPS)
            else:
                w = a["w_kv"].rearrange("(k p) (c g n) -> c g p k n", p=P, c=2, g=GROUPS)[u]
            return w[later:][bass.ds(g, 1), :, 4 * part:4 * part + 4, cols].rearrange("o p k n -> p (o k) n")

        def sp_project(sp):
            S = ffn[0]
            sp.wait_ge(S.gl, NF)
            sp.wait_ge(S.hi, 6 * NB)
            sp.wait_ge(S.lo, 6 * NB)
            sp.dma_start(rot[:, :, :, :], a["rot"]).then_inc(rows_out[0], 16)
            sp.dma_start(hg[:, 0, :], a["k_gain"].partition_broadcast(P)).then_inc(rows_out[1], 16)
            sp.dma_start(hg[:, 1, :], a["q_gain"][0].partition_broadcast(P)).then_inc(rows_out[2], 16)

            def load(m, g, free=False):
                src = pj_src(m % 12 // 4, m % 4 // 2, m % 2, g, m // 12)
                if m >= 3 and not free:
                    sp.wait_ge(pj_l, 12 * g + (m - 2))
                sp.dma_start(stage[:, m % 3, :].rearrange("p (k n) -> p k n", k=4), src).then_inc(piece_in[m % 3], 16)

            def body(g, last):
                for u in range(3):
                    for t in range(9):
                        G = 27 * g + 9 * u + t
                        M = MT[t]
                        if u == 0 and t == 5:
                            sp.wait_ge(pj_l, 12 * g + 6)
                        if u == 1:
                            sp.wait_ge(pj_v, G + (K0 + 1))
                        else:
                            sp.wait_ge(pj_r, 5 * (18 * g + (9 if u else 0) + t + 1))
                        rows = slice(t * P, t * P + M)
                        dst = qs[bass.ds(g, 1), rows, :] if u == 2 else kvs[bass.ds(g, 1), rows, u, :]
                        sp.dma_start(dst.rearrange("o p n -> (o p) n"), kn[0:M, t % 3, :]).then_inc(rows_out[t % 3], 16)
                        for m in {2: [4 * u + 7], 5: [4 * u + 8], 8: [4 * u + 9, 4 * u + 10]}.get(t, []):
                            if m < 12 or not last:
                                load(m, g, free=(m == 8))

            for m in range(7):
                load(m, 0)
            with sp.Fori(0, GROUPS - 1) as g:
                body(g, False)
            body(GROUPS - 1, True)

        def pj_piece(e, g, m, act):
            u, H, part = m % 12 // 4, m // 2, m % 2
            gain = G_ATTN if u == 2 else G_KV
            if act:
                e.wait_ge(piece_in[m % 3], 64 * g + 16 * (m // 3 + 1))
                if H % 2:
                    wait(e, pj_half, 3 * g + (H - 1) // 2)
                else:
                    wait(e, pj_pe, 27 * g + (9 * ((H - 3) // 2 + 1) + 1))
            else:
                e.wait_ge(pj_h, 12 * g + m + 1)
            for i in range(4):
                k = 4 * part + i
                w = stage[:, m % 3, i * HW:(i + 1) * HW]
                sc_ = gT[:, gain + k:gain + k + 1]
                if act:
                    ins = nc.scalar.activation(wph[H % 3][:, k, :], w, ACT.Copy, scale=sc_)
                else:
                    ins = nc.vector.scalar_tensor_tensor(out=wpl[H % 3][:, k, :], in0=w, scalar=sc_,
                                                         in1=wph[H % 3][:, k, :].bitcast(F32), op0=ALU.mult, op1=ALU.subtract)
            ins.then_inc(pj_h if act else pj_l, 1)

        def pieces_at(u, t, last):
            if u == 2 and last:
                return []
            return {3: [4 * u + 4], 5: [4 * u + 5], 7: [4 * u + 6, 4 * u + 7]}.get(t, [])

        def act_project(act):
            for m in range(2, 4):
                pj_piece(act, 0, m, True)
            act.wait_ge(pj_v, 1)
            act.wait_ge(pj_s, 1)
            nc.scalar.activation(rtok[:, :], rtmp[:, 0, :], ACT.Sqrt).then_inc(pj_a, 1)

            def body(g, last):
                for u in range(3):
                    for t in range(9):
                        for m in pieces_at(u, t, last):
                            pj_piece(act, g, m, True)
                        M, G = MT[t], 27 * g + 9 * u + t
                        if u != 1:
                            Q = 18 * g + (9 if u else 0) + t
                            act.wait_ge(pj_pe, G + 1)
                            act.wait_ge(pj_v, K0)
                            act.wait_ge(pj_s, 7 * Q + 1)
                            nc.scalar.activation(sq[0:M, 0, 0:QW], ps[0:M, t % 3, :], ACT.Square,
                                                 scale=rtok[0:M, t:t + 1]).then_inc(pj_sq, 1)
                            act.wait_ge(pj_s, 7 * Q + 3)
                            nc.scalar.activation(hs[0:M, 2, :], hs[0:M, 1, :], ACT.Sqrt).then_inc(pj_rt, 1)

            with act.Fori(0, GROUPS - 1) as g:
                body(g, False)
            body(GROUPS - 1, True)

        def dve_project(v):
            for m in range(2, 4):
                pj_piece(v, 0, m, False)
            v.wait_ge(pj_n, 1)
            nc.vector.tensor_scalar(rtmp[:, 0, 0:8], ps[:, 7, 0:8], 1.0 / D, EPS, ALU.mult, ALU.add).then_inc(pj_v, 1)
            nc.vector.tensor_scalar(rtmp[0:NS, 0, 8:9], ps[0:NS, 7, 8:9], 1.0 / D, EPS, ALU.mult, ALU.add).then_inc(pj_s, 1)
            newton(v, rtmp[:, 0, :], rtok[:, :], rtmp[:, 2, :], pj_v, 1, pj_a, 1)

            def body(g, last):
                for u in range(3):
                    for t in range(9):
                        for m in pieces_at(u, t, last):
                            pj_piece(v, g, m, False)
                        M, G = MT[t], 27 * g + 9 * u + t
                        b = t % 3
                        v.wait_ge(rows_out[b], 144 * g + 16 * (3 * u + t // 3 + 1))
                        if u == 1:
                            v.wait_ge(pj_pe, G + 1)
                            nc.vector.tensor_scalar(kn[0:M, b, :], ps[0:M, b, :], rtok[0:M, t:t + 1], None,
                                                    ALU.mult).then_inc(pj_v, 1)
                        else:
                            Q = 18 * g + (9 if u else 0) + t
                            ms, m_, y, tt, f = (hs[0:M, i, :] for i in range(5))
                            v.wait_ge(pj_sq, Q + 1)
                            nc.vector.tensor_reduce(ms, sq[0:M, 0, 0:QW].rearrange("p (h e) -> p h e", h=HEADS), AX.X,
                                                    ALU.add).then_inc(pj_s, 1)
                            v.wait_ge(pj_s, 7 * Q + 2)
                            nc.vector.tensor_scalar(m_, ms, 1.0 / HD, EPS, ALU.mult, ALU.add).then_inc(pj_s, 1)
                            newton(v, m_, y, tt, pj_s, 7 * Q + 3, pj_rt, Q + 1)
                            nc.vector.tensor_scalar(f, y, rtok[0:M, t:t + 1], 0.125 if u else 1.0, ALU.mult,
                                                    ALU.mult).then_inc(pj_s, 1)
                            v.wait_ge(pj_s, 7 * Q + 8)
                            nc.vector.tensor_tensor(kn[0:M, b, :].rearrange("p (h e) -> p h e", h=HEADS),
                                                    ps[0:M, b, :].rearrange("p (h e) -> p h e", h=HEADS),
                                                    f.unsqueeze(2).to_broadcast([M, HEADS, HD]), ALU.mult).then_inc(pj_v, 1)

            with v.Fori(0, GROUPS - 1) as g:
                body(g, False)
            body(GROUPS - 1, True)

        def pool_project(q):
            for i in range(3):
                q.wait_ge(rows_out[i], 16)
            half = HEADS * 8
            with q.Fori(0, GROUPS) as g:
                for u in (0, 2):
                    for t in range(9):
                        M, G, b = MT[t], 27 * g + 9 * u + t, t % 3
                        n = 5 * (18 * g + (9 if u else 0) + t)
                        row = kn[0:M, b, :].rearrange("p (h e) -> p h e", h=HEADS)
                        t1 = sq[0:M, 1, 0:2 * half].rearrange("p (h e) -> p h e", h=HEADS)
                        t2 = sq[0:M, 1, 2 * half:4 * half].rearrange("p (h e) -> p h e", h=HEADS)

                        def per_head(tab, w):
                            return tab.unsqueeze(1).to_broadcast([M, HEADS, w])
                        q.wait_ge(pj_v, G + (K0 + 1))
                        nc.gpsimd.tensor_tensor(row, row, per_head(hg[0:M, 1 if u else 0, :], HD), ALU.mult).then_inc(pj_r, 1)
                        q.wait_ge(pj_r, n + 1)
                        nc.gpsimd.tensor_tensor(t1, row[:, :, 0:16], per_head(rot[0:M, 0, t, :], 16), ALU.mult).then_inc(pj_r, 1)
                        nc.gpsimd.tensor_tensor(t2[:, :, 0:8], row[:, :, 8:16], per_head(rot[0:M, 1, t, 0:8], 8),
                                                ALU.mult).then_inc(pj_r, 1)
                        nc.gpsimd.tensor_tensor(t2[:, :, 8:16], row[:, :, 0:8], per_head(rot[0:M, 1, t, 8:16], 8),
                                                ALU.mult).then_inc(pj_r, 1)
                        q.wait_ge(pj_r, n + 4)
                        nc.gpsimd.tensor_tensor(row[:, :, 0:16], t1, t2, ALU.add).then_inc(pj_r, 1)

        def pe_project(pe):
            order = [(t, h) for t in range(7) for h in range(2)] + [(7, 0), (8, 0), (7, 1), (8, 1)]

            def body(g, first):
                for u in range(3):
                    for t, h in order:
                        start = first and u == 0
                        M, G, tok = MT[t], 27 * g + 9 * u + t, slice(t * P, t * P + MT[t])
                        if h == 0 and not (start and t < 3):
                            pe.wait_ge(pj_v, G + (K0 - 2))
                        W, Wt = wph[(2 * u + h) % 3], wpl[(2 * u + h) % 3]
                        for k in range(KC):
                            if t == 0 and k % 4 == 0:
                                pe.wait_ge(pj_l, 12 * g + 4 * u + 2 * h + k // 4 + 1)
                            if start and t == 0 and h == 0:
                                pe.wait_ge(split_lo, split[1].lo + k + 1)
                            out = ps[0:M, t % 3, h * HW:(h + 1) * HW]
                            pe.matmul(out, xh[:, k, tok], W[:, k, :], start=(k == 0), stop=False)
                            pe.matmul(out, xh[:, k, tok], Wt[:, k, :], start=False, stop=False)
                            mm = pe.matmul(out, xl[:, k, tok], W[:, k, :], start=False, stop=(k == KC - 1))
                        if h == 1:
                            mm.then_inc(pj_pe, 1)
                        elif t == 8:
                            mm.then_inc(pj_half, 1)
                        if start and t == 0 and h == 1:
                            pe.wait_ge(split_acc, split[1].acc + KC - 1)
                            pe.wait_ge(ffn[0].ct, NF // 2)
                            for i in range(9):
                                mm = pe.matmul(ps[0:MT[i], 7, i:i + 1], acc[:, i * P:i * P + MT[i]], ones[:, 0:1],
                                               start=True, stop=True)
                            mm.then_inc(pj_n, 1)

            pe.wait_ge(ffn[0].A, 6 * LAST + 6)
            body(0, True)
            with pe.Fori(1, GROUPS) as g:
                body(g, False)

        STEPS = [(0, n, 0, n > 0) for n in range(8)] + [(1, n, r, n > 0) for r in range(4) for n in range(2)] + \
            [(2, s, 0, False) for s in range(8)]
        ROWS = 16 + 16 * 9 * GROUPS
        NSTEP, NH = len(STEPS), 2 * len(STEPS)

        def tile_rows(src, s):
            g, n, r, _ = STEPS[s]
            if g == 0:
                return [(slice(0, P), src[n * P:(n + 1) * P, :])]
            if g == 1:
                return [(slice(0, P), src.rearrange("(m r) c -> r m c", r=4)[r, n * P:(n + 1) * P, :])]
            v = src.rearrange("(u r) c -> r u c", r=16)
            return [(slice(64 * e, 64 * e + 64), v[2 * n + e]) for e in range(2)]

        def dmas(s):
            return 2 if STEPS[s][0] == 2 else 1

        def moved(s, ring):
            return 16 * sum(dmas(i) for i in range(s % ring, s + 1, ring))

        def wide(i):
            return STEPS[i // 2][3]

        def span(i):
            return 2 * P if wide(i) else P

        def wides(i):
            return sum(wide(n) for n in range(i + 1))

        KEYS = (P, P, 64)
        CACHES = ("cache_kv_w128", "cache_kv_w512", "cache_kv_w2048")
        ST = 3 * NS
        H_SC, H_NEW, H_SM = 3, 28, 33

        WIN = (128, 512, T)
        KV_PARTS = [(g, r, min(P, N - r), name) for g, name in enumerate(("kv_w128", "kv_w512", "kv_w2048"))
                    for r in range(T - WIN[g], N, P)]

        def sp_attention(sp):
            sp.wait_ge(pj_pe, 27 * GROUPS)
            sp.wait_ge(pj_h, 12 * GROUPS)
            sp.wait_ge(pj_l, 12 * GROUPS)
            for i in range(3):
                sp.wait_ge(rows_out[i], ROWS)

            def load_q(s):
                if s >= 2:
                    sp.wait_ge(at_tp, 2 * s - 3)
                for part, src in tile_rows(qs[STEPS[s][0], 0:T], s):
                    sp.dma_start(qt[part, s % 2, :], src).then_inc(at_q[s % 2], 16)

            def load_kv(s):
                if s >= 4:
                    sp.wait_ge(at_o, 2 * s - 4 if STEPS[s - 3][3] else 2 * s - 6)
                for part, src in tile_rows(kvs[STEPS[s][0], 0:T].rearrange("t c n -> t (c n)"), s):
                    sp.dma_start(kvt[part, s % 4, :], src).then_inc(at_kv[s % 4], 16)

            def load_sample(n):
                s, g = n // 3, n % 3
                if g == 0:
                    if s >= 2:
                        sp.wait_ge(sm_p, n - 3)
                    sp.dma_start(qb[:, s % 2, :, :], qs[:, T + s, :].partition_broadcast(P)).then_inc(sm_q[s % 2], 16)
                if n >= 3:
                    sp.wait_ge(sm_p, n - 2)
                sp.dma_start(kc[0:KEYS[g], n % 3, :], a[CACHES[g]][s, ::DIL[g], 0].rearrange(
                    "t h e -> t (h e)")).then_inc(sm_k[n % 3], 16)

            load_q(0)
            load_kv(0)
            load_q(1)
            sp.dma_start(maskf[:, :, :], a["masks"]).then_inc(in_mask, 16)
            for g in range(GROUPS):
                sp.dma_start(qn[:, g, :], qs[g, T:N, :]).then_inc(in_new, 16)
                sp.dma_start(stage[0:NS, g, :], kvs[g, T:N].rearrange("t c n -> t (c n)")).then_inc(in_new, 16)
            sp.dma_start(samp[:, :], a["samp"]).then_inc(in_new, 16)
            for s in range(NSTEP + 3):
                if 1 <= s < NSTEP:
                    if s + 1 < NSTEP:
                        load_q(s + 1)
                    load_kv(s)
                if s >= 3:
                    store_o(sp, s - 3)
                for n in (2 * s - 4, 2 * s - 3):
                    if 0 <= n < ST:
                        load_sample(n)
                if 4 <= s < 4 + len(KV_PARTS):
                    g, first, rows, name = KV_PARTS[s - 4]
                    dst = (o[name + "_prompt"][0] if first < T else o[name + "_sample"][:, 0]).rearrange("t c h e -> t c (h e)")
                    at = first - (T - WIN[g]) if first < T else 0
                    sp.dma_start(dst[at:at + rows], kvs[g, first:first + rows]).then_inc(kv_out, 16)
                if s == 17:
                    sp.wait_ge(sm_p, ST)
                    sp.dma_start(diag, a["diag"]).then_inc(in_diag, 16)
                    for n in range(3):
                        load_v(sp, n)
                for n in {20: [3], 21: [4, 5], 22: [6], 23: [7]}.get(s, []):
                    load_v(sp, n)

        def values_of(s):
            return vc[:, :, :] if s % 3 == 0 else qb[:, s % 3 - 1, :, :]

        def load_v(e, s):
            if s >= 3:
                e.wait_ge(sm_o, 3 * (s - 2))
            for g in range(GROUPS):
                e.dma_start(values_of(s)[0:KEYS[g], g, :], a[CACHES[g]][s, ::DIL[g], 1].rearrange(
                    "t h e -> t (h e)")).then_inc(sm_vin[s % 3], 16)

        def value_step(i):
            n = i - H_SM - 3
            return {0: 0, 1: 1, 2: 2, 3: 3, 5: 4, 6: 5, 7: 6, 8: 7}.get(n), {4: 0, 9: 1}.get(n)

        def store_o(e, s):
            e.wait_ge(at_oc, 2 * s + 2)
            e.wait_ge(at_e, 2 * s + 2)
            for part, dst in tile_rows(os_[STEPS[s][0]], s):
                e.dma_start(dst, osb[part, s % 3, :]).then_inc(rows_out[s % 3], 16)

        def scores_out(i):
            b = 2 * (i % 2)
            return ps[:, b:b + 2, 0:2 * span(i)].rearrange("p b (h n) -> p b h n", h=2)

        def pe_attention(pe):
            def turn(tile, s):
                for hp in range(4):
                    mm = pe.transpose(ps[:, 7, hp * P:(hp + 1) * P], tile[:, hp * P:(hp + 1) * P], ident[:, :])
                mm.then_inc(at_tp, 1)

            def turn_q(s):
                pe.wait_ge(at_q[s % 2], moved(s, 2))
                wait(pe, at_tc, 2 * s)
                turn(qt[:, s % 2, :], s)

            def turn_k(s):
                pe.wait_ge(at_kv[s % 4], moved(s, 4))
                pe.wait_ge(at_tc, 2 * s + 1)
                turn(kvt[:, s % 4, 0:QW], s)

            def scores(i):
                s, half = i // 2, i % 2
                b = 2 * (i % 2)
                pe.wait_ge(at_tc, 2 * s + 2)
                if i >= 2:
                    pe.wait_ge(at_e, i - 1)
                if i == 0:
                    pe.wait_ge(at_mk, 4)
                m = 0 if wide(i) else (2 if STEPS[s][0] == 2 else 1)
                for c in range(2):
                    pe.matmul(ps[:, b + c, 0:2 * span(i)], identb[:, :], mask[:, m, 0:2 * span(i)], start=True, stop=True)
                slots = [(s - 1) % 3, s % 3] if wide(i) else [s % 3]
                for pair in range(2):
                    for w, slot in enumerate(slots):
                        for odd in range(2):
                            part = slice(64 * odd, 64 * odd + 64)
                            hp = 2 * half + pair
                            at = pair * span(i) + w * P
                            mm = pe.matmul(ps[:, b + odd, at:at + P], qT[part, s % 2, hp * P:(hp + 1) * P],
                                           kT[part, slot, hp * P:(hp + 1) * P], start=False, stop=True,
                                           skip_group_check=True)
                mm.then_inc(at_s, 1)

            def turn_p(i):
                pe.wait_ge(at_e, i + 1)
                if i:
                    pe.wait_ge(at_pa, i)
                wait(pe, at_pb, wides(i - 1))
                for n in range(8 if wide(i) else 4):
                    mm = pe.transpose(ps[:, 4 + n // 4, n % 4 * P:(n % 4 + 1) * P], prob[:, i % 2, n * P:(n + 1) * P],
                                      ident[:, :])
                mm.then_inc(at_pt, 1)

            def outputs(i):
                s = i // 2
                pe.wait_ge(at_pa, i + 1)
                wait(pe, at_pb, wides(i))
                if i:
                    pe.wait_ge(at_oc, i)
                for j in range(4):
                    h = 4 * (i % 2) + j
                    tiles = [(s - 1) % 4, s % 4] if wide(i) else [s % 4]
                    for w, slot in enumerate(tiles):
                        n = j * len(tiles) + w
                        v = kvt[:, slot, QW + h // 2 * P:QW + (h // 2 + 1) * P]
                        mm = pe.matmul(ps[:, 6, j * P:(j + 1) * P], probT[:, i % 2, n * P:(n + 1) * P], v,
                                       start=(w == 0), stop=(w == len(tiles) - 1))
                mm.then_inc(at_o, 1)

            def values(s):
                pe.wait_ge(sm_vin[s % 3], 48 * (s // 3 + 1))
                if s == 0:
                    pe.wait_ge(sm_st, 7)
                if s == 4:
                    pe.wait_ge(sm_st, 13)
                for g in range(GROUPS):
                    pe.matmul(ps[32 * (s % 4):32 * (s % 4) + 32, 5, :],
                              pT[0:KEYS[g], (g * NS + s) * 32:(g * NS + s + 1) * 32], values_of(s)[0:KEYS[g], g, :],
                              start=(g == 0), stop=(g == GROUPS - 1), tile_position=(0, 32 * (s % 4))).then_inc(sm_o, 1)

            turn_q(0)
            turn_k(0)
            for i in range(NH + 2):
                if i < NH:
                    scores(i)
                if i // 2 + 1 < NSTEP:
                    (turn_k if i % 2 else turn_q)(i // 2 + 1)
                if 0 < i <= NH:
                    turn_p(i - 1)
                if i >= 2:
                    outputs(i - 2)
                if i == H_SM:
                    pe.wait_ge(at_pb, wides(NH - 1))
                    pe.wait_ge(sm_r, ST)
                    pe.wait_ge(sm_new, 9)
                    for g in range(GROUPS):
                        pe.transpose(ps[0:64, 5, g * P:g * P + KEYS[g]], sc[0:KEYS[g], g * 64:(g + 1) * 64],
                                     ident[0:KEYS[g], 0:KEYS[g]])
                    for g in range(GROUPS):
                        mm = pe.matmul(ps[0:64, 5, SK - 3 + g:SK - 2 + g], bnew[:, g * 64:(g + 1) * 64], ones[0:NS, 0:1],
                                       start=True, stop=True)
                    mm.then_inc(sm_pe, 1)
                if i == H_SM + 2:
                    pe.wait_ge(sm_st, 3)
                    for g in range(GROUPS):
                        mm = pe.transpose(ps[0:KEYS[g], 5, g * 64:(g + 1) * 64], sall[:, g * P:g * P + KEYS[g]],
                                          ident[0:64, 0:64])
                    mm.then_inc(sm_pe, 1)
                    pe.wait_ge(sm_st, 4)
                    pe.matmul(ps[0:NS, 5, 448:472], sel8, an, start=True, stop=True).then_inc(sm_pe, 1)
                sample, _ = value_step(i)
                if sample is not None:
                    values(sample)

        def dve_attention(v):
            v.wait_ge(in_mask, 16)
            nc.vector.tensor_copy(identb[:, :], ident[:, :]).then_inc(at_mk, 1)
            for m in range(3):
                if m == 0:
                    ins = nc.vector.tensor_copy(mask[:, 0, :].rearrange("p (w n) -> p w n", w=2),
                                                maskf[:, 0:2, :].rearrange("p c n -> p (c n)").unsqueeze(1).to_broadcast([P, 2, 2 * P]))
                else:
                    ins = nc.vector.tensor_copy(mask[:, m, 0:2 * P].rearrange("p (w n) -> p w n", w=2),
                                                maskf[:, m, :].unsqueeze(1).to_broadcast([P, 2, P]))
                ins.then_inc(at_mk, 1)

            def turned(s, k):
                v.wait_ge(at_tp, 2 * s + 1 + k)
                nc.vector.tensor_copy(kT[:, s % 3, :] if k else qT[:, s % 2, :], ps[:, 7, :]).then_inc(at_tc, 1)

            def maxima(i):
                s = i // 2
                v.wait_ge(at_s, i + 1)
                if s >= 3:
                    v.wait_ge(rows_out[s % 3], ROWS + moved(s - 3, 3))
                dst = osb[:, s % 3, QW + 4 * (i % 2):QW + 4 * (i % 2) + 4].rearrange("p (h b) -> p b h", b=2)
                nc.vector.tensor_reduce(dst, scores_out(i), AX.X, ALU.max, negate=True).then_inc(at_m, 1)

            def probs(i):
                v.wait_ge(at_pt, i + 1)
                nc.vector.tensor_copy(probT[:, i % 2, 0:512], ps[:, 4, :]).then_inc(at_pa, 1)

            def outs(i):
                v.wait_ge(at_o, i + 1)
                src = ps[:, 6, :].rearrange("p (q o) -> p q o", q=2)
                dst = osb[:, i // 2 % 3, 256 * (i % 2):256 * (i % 2) + 256].rearrange("p (q o) -> p q o", q=2)
                nc.vector.tensor_copy(dst[:, :, 0:64], src[:, :, 0:64])
                nc.vector.tensor_copy(dst[:, :, 64:128], src[:, :, 192:256]).then_inc(at_oc, 1)

            turned(0, 0)
            turned(0, 1)
            for i in range(NH + 2):
                if i < NH:
                    maxima(i)
                if i // 2 + 1 < NSTEP:
                    turned(i // 2 + 1, i % 2)
                if 0 < i <= NH:
                    probs(i - 1)
                if i >= 2:
                    outs(i - 2)
                if 0 <= i - H_SC < ST:
                    n = i - H_SC
                    s, g = n // 3, n % 3
                    v.wait_ge(sm_p, n + 1)
                    nc.vector.tensor_reduce(sc[0:KEYS[g], g * 64 + s * 8:g * 64 + s * 8 + 8],
                                            prod[0:KEYS[g], 0, :].rearrange("p (h e) -> p h e", h=HEADS), AX.X,
                                            ALU.add).then_inc(sm_r, 1)
                if i == H_NEW:
                    dve_new_keys(v)
                if i == H_SM:
                    v.wait_ge(sm_pe, 1)
                    nc.vector.tensor_reduce(stat[:, 0:1], ps[0:64, 5, 0:SK], AX.X, ALU.max, negate=True).then_inc(sm_st, 1)
                if i == H_SM + 1:
                    v.wait_ge(sm_e, 1)
                    nc.vector.reciprocal(stat[:, 2:3], stat[:, 1:2]).then_inc(sm_st, 1)
                    v.wait_ge(sm_st, 2)
                    nc.vector.tensor_scalar(sall, sall, stat[:, 2:3], None, ALU.mult).then_inc(sm_st, 1)
                    v.wait_ge(sm_st, 3)
                    nc.vector.tensor_tensor(an.rearrange("p (g h) -> p g h", g=GROUPS),
                                            del8.unsqueeze(1).to_broadcast([64, GROUPS, HEADS]),
                                            sall[:, SK - 3:SK].unsqueeze(2).to_broadcast([64, GROUPS, HEADS]),
                                            ALU.mult).then_inc(sm_st, 1)
                if i == H_SM + 2:
                    dve_sample_probs(v)
                _, four = value_step(i)
                if four is not None:
                    if four == 0:
                        v.wait_ge(in_diag, 16)
                        v.wait_ge(sm_st, 12)
                    v.wait_ge(sm_o, 12 * (four + 1))
                    nc.vector.tensor_tensor((om1, om2)[four], ps[:, 5, :], diag, ALU.mult).then_inc(sm_st, 1)

        def dve_new_keys(v):
            v.wait_ge(in_new, 16 * 7)
            v.wait_ge(sm_z, 1)
            tmp = om1[0:NS, :]
            for g in range(GROUPS):
                wait(v, sm_new, 2 * g)
                nc.vector.tensor_tensor(tmp, qn[:, g, :], stage[0:NS, g, 0:QW], ALU.mult).then_inc(sm_new, 1)
                v.wait_ge(sm_new, 2 * g + 1)
                nc.vector.tensor_reduce(snew[:, g * 8:g * 8 + 8], tmp.rearrange("p (h e) -> p h e", h=HEADS), AX.X,
                                        ALU.add).then_inc(sm_new, 1)
            v.wait_ge(sm_new, 6)
            for g in range(GROUPS):
                nc.vector.tensor_tensor(bnew[:, g * 64:(g + 1) * 64].rearrange("p (s h) -> p s h", s=NS),
                                        del64.rearrange("p (s h) -> p s h", s=NS),
                                        snew[:, g * 8:g * 8 + 8].unsqueeze(1).to_broadcast([NS, NS, HEADS]),
                                        ALU.mult).then_inc(sm_new, 1)

        def dve_sample_probs(v):
            v.wait_ge(sm_pe, 3)
            v.wait_ge(sm_z, 1)
            for part, g0, g1 in ((P, 0, 2), (64, 2, 3)):
                nc.vector.tensor_copy(pT[0:part, g0 * 256:g1 * 256].rearrange("p (s w) -> p s w", w=32)[:, :, 0:HEADS],
                                      ps[0:part, 5, g0 * 64:g1 * 64].rearrange("p (s w) -> p s w", w=HEADS)).then_inc(sm_st, 1)
            nc.vector.tensor_copy(pnew, ps[0:NS, 5, 448:472]).then_inc(sm_st, 1)
            v.wait_ge(sm_st, 7)

            def part(dst, g):
                nc.vector.tensor_tensor(dst.rearrange("p (h e) -> p h e", h=HEADS),
                                        stage[0:NS, g, QW:2 * QW].rearrange("p (h e) -> p h e", h=HEADS),
                                        pnew[:, g * 8:g * 8 + 8].unsqueeze(2).to_broadcast([NS, HEADS, HD]),
                                        ALU.mult).then_inc(sm_st, 1)
            tmp = om1[0:NS, :]
            part(onew, 0)
            for g in range(1, GROUPS):
                part(tmp, g)
                v.wait_ge(sm_st, 7 + 2 * g)
                nc.vector.tensor_tensor(onew, onew, tmp, ALU.add).then_inc(sm_st, 1)
                v.wait_ge(sm_st, 8 + 2 * g)

        def act_attention(act):
            for i in range(NH + 2):
                if i < NH:
                    s, n = i // 2, span(i)
                    act.wait_ge(at_m, i + 1)
                    if i >= 2:
                        act.wait_ge(at_pt, i - 1)
                    src = scores_out(i)
                    for j in range(4):
                        h = 4 * (i % 2) + j
                        ins = nc.scalar.activation(prob[:, i % 2, j * n:(j + 1) * n], src[:, j % 2, j // 2, :], ACT.Exp,
                                                   bias=osb[:, s % 3, QW + h:QW + h + 1],
                                                   accum_out=osb[:, s % 3, QW + HEADS + h:QW + HEADS + h + 1])
                    ins.then_inc(at_e, 1)
                if 0 < i <= NH and wide(i - 1):
                    act.wait_ge(at_pt, i)
                    nc.scalar.activation(probT[:, (i - 1) % 2, 512:1024], ps[:, 5, :], ACT.Copy).then_inc(at_pb, 1)
                if i == H_SM:
                    act.wait_ge(sm_st, 1)
                    nc.scalar.activation(sall, ps[0:64, 5, 0:SK], ACT.Exp, bias=stat[:, 0:1],
                                         accum_out=stat[:, 1:2]).then_inc(sm_e, 1)

        def pool_attention(q):
            q.wait_ge(pj_r, 5 * 18 * GROUPS)
            q.wait_ge(pj_s, 1 + 7 * 18 * GROUPS)
            nc.gpsimd.memset(pT, 0.0).then_inc(sm_z, 1)
            for n in range(ST):
                s, g = n // 3, n % 3
                if g == 0:
                    q.wait_ge(sm_q[s % 2], 16 * (s // 2 + 1))
                q.wait_ge(sm_k[n % 3], 16 * (n // 3 + 1))
                wait(q, sm_r, n)
                nc.gpsimd.tensor_tensor(prod[0:KEYS[g], 0, :], kc[0:KEYS[g], n % 3, :], qb[0:KEYS[g], s % 2, g, :],
                                        ALU.mult).then_inc(sm_p, 1)

        MG = 6

        def sp_merge(sp):
            for i in range(3):
                sp.wait_ge(rows_out[i], ROWS + moved(NSTEP - 3 + i, 3))
            sp.wait_ge(at_o, NH)

            def load(t):
                if t >= 4:
                    sp.wait_ge(mg_pe, t - 3)
                sp.dma_start(om[:, t % 4, :, :], os_[:, t * P:(t + 1) * P, :].rearrange("g p c -> p g c")).then_inc(
                    mg_in[t % 4], 16)

            def load_wo(k):
                if k == 0:
                    sp.wait_ge(sm_st, 12)
                if k == 3:
                    sp.wait_ge(wo_h, 1)
                    sp.wait_ge(wo_l, 1)
                sp.dma_start(stage[:, k % 3, :], a["w_o"][0, k * P:(k + 1) * P, :]).then_inc(piece_in[k % 3], 16)

            for t in range(8):
                load(t)
                if 2 <= t < 6:
                    load_wo(t - 2)

        def dve_merge(v):
            def first(t):
                b = t % 2
                nm = om[:, t % 4, :, QW:QW + HEADS]
                v.wait_ge(mg_in[t % 4], 16 * (t // 4 + 1))
                if t >= 2:
                    v.wait_ge(mg_p, t - 1)
                    v.wait_ge(mg_v, MG * (t - 1))
                nc.vector.tensor_reduce(ow[:, b, 0, 0:8], nm.rearrange("p g h -> p h g"), AX.X, ALU.min).then_inc(mg_a, 1)
                v.wait_ge(mg_a, 2 * t + 1)
                nc.vector.tensor_tensor(ow[:, b, 1, :].rearrange("p (g h) -> p g h", g=GROUPS),
                                        ow[:, b, 0, 0:8].unsqueeze(1).to_broadcast([P, GROUPS, HEADS]), nm,
                                        ALU.subtract).then_inc(mg_a, 1)

            def weighted(dst, src, w, h=HEADS):
                return dict(out=dst.rearrange("p (h e) -> p h e", h=h), in0=src.rearrange("p (h e) -> p h e", h=h),
                            in1=w.unsqueeze(2).to_broadcast([P, h, HD]), op=ALU.mult)

            def second(t):
                b, n = t % 2, MG * t
                den = om[:, t % 4, :, QW + HEADS:OW]
                three_g = dict(g=GROUPS)
                e, ed, w = (ow[:, b, i, :] for i in (1, 2, 3))
                v.wait_ge(mg_e, t + 1)
                nc.vector.tensor_tensor(ed.rearrange("p (g h) -> p g h", **three_g), e.rearrange("p (g h) -> p g h", **three_g),
                                        den, ALU.mult).then_inc(mg_v, 1)
                v.wait_ge(mg_v, n + 1)
                nc.vector.tensor_reduce(ow[:, b, 0, 8:16], ed.rearrange("p (g h) -> p h g", **three_g), AX.X,
                                        ALU.add).then_inc(mg_v, 1)
                v.wait_ge(mg_v, n + 2)
                nc.vector.reciprocal(ow[:, b, 0, 16:24], ow[:, b, 0, 8:16]).then_inc(mg_v, 1)
                v.wait_ge(mg_v, n + 3)
                nc.vector.tensor_tensor(w.rearrange("p (g h) -> p g h", **three_g), e.rearrange("p (g h) -> p g h", **three_g),
                                        ow[:, b, 0, 16:24].unsqueeze(1).to_broadcast([P, GROUPS, HEADS]),
                                        ALU.mult).then_inc(mg_v, 1)
                v.wait_ge(mg_v, n + 4)
                if t >= 2:
                    v.wait_ge(mg_pe, t - 1)
                nc.vector.tensor_tensor(**weighted(ot[:, b, 0, :], om[:, t % 4, 0, 0:QW], w[:, 0:8])).then_inc(mg_v, 1)
                nc.vector.tensor_tensor(**weighted(ot[:, b, 1, :], om[:, t % 4, 2, 0:QW], w[:, 16:24])).then_inc(mg_v, 1)

            def lo(t):
                v.wait_ge(mg_h, t + 1)
                nc.vector.tensor_tensor(oTl[:, :, t * P:(t + 1) * P], ps[:, 6 + t % 2, :].rearrange("p (c n) -> p c n", c=4),
                                        oTh[:, :, t * P:(t + 1) * P].bitcast(F32), ALU.subtract).then_inc(mg_l, 1)

            def split_wo(k):
                v.wait_ge(wo_h, k + 1)
                nc.vector.tensor_tensor(wol[:, k, :], stage[:, k % 3, :], woh[:, k, :].bitcast(F32), ALU.subtract).then_inc(wo_l, 1)

            v.wait_ge(sm_fh, 1)
            nc.vector.tensor_tensor(oTl[:, :, T:N], ps[:, 5, 0:4 * NS].rearrange("p (c s) -> p c s", c=4),
                                    oTh[:, :, T:N].bitcast(F32), ALU.subtract).then_inc(sm_fl, 1)
            first(0)
            for t in range(8):
                if t < 7:
                    first(t + 1)
                second(t)
                if t:
                    lo(t - 1)
                if 2 < t < 7:
                    split_wo(t - 3)
            lo(7)
            for d in range(KC):
                v.wait_ge(wo_pe, d + 1)
                nc.vector.tensor_tensor(cols3(x[:, d, :]), cols3(x[:, d, :]), bank3(d % 2), ALU.add).then_inc(wo_x, 1)
                if d:
                    dve_split(v, split[2], d - 1, G_FFN + KC)
            dve_split(v, split[2], KC - 1, G_FFN + KC)
            dve_ffn_slab0(v, ffn[1])

        def pool_merge(q):
            for t in range(8):
                b = t % 2
                q.wait_ge(mg_v, MG * t + 4)
                row = om[:, t % 4, 1, 0:QW].rearrange("p (h e) -> p h e", h=HEADS)
                nc.gpsimd.tensor_tensor(row, row, ow[:, b, 3, 8:16].unsqueeze(2).to_broadcast([P, HEADS, HD]),
                                        ALU.mult).then_inc(mg_p, 1)

        def act_merge(act):
            def exps(t):
                b = t % 2
                act.wait_ge(mg_a, 2 * t + 2)
                nc.scalar.activation(ow[:, b, 1, :], ow[:, b, 1, :], ACT.Exp).then_inc(mg_e, 1)

            def hi(t):
                act.wait_ge(mg_pe, t + 1)
                nc.scalar.activation(oTh[:, :, t * P:(t + 1) * P], ps[:, 6 + t % 2, :].rearrange("p (c n) -> p c n", c=4),
                                     ACT.Copy).then_inc(mg_h, 1)
            act.wait_ge(sm_f, 1)
            nc.scalar.activation(oTh[:, :, T:N], ps[:, 5, 0:4 * NS].rearrange("p (c s) -> p c s", c=4),
                                 ACT.Copy).then_inc(sm_fh, 1)
            act.wait_ge(sm_o, ST)

            def split_wo(k):
                act.wait_ge(piece_in[k % 3], 64 * GROUPS + 16 * (k // 3 + 1))
                nc.scalar.activation(woh[:, k, :], stage[:, k % 3, :], ACT.Copy).then_inc(wo_h, 1)

            for t in range(8):
                exps(t)
                if t:
                    hi(t - 1)
                if 2 < t < 7:
                    split_wo(t - 3)
            hi(7)
            act.wait_ge(wo_l, 4)
            for d in range(KC):
                act.wait_ge(wo_x, d + 1)
                act_split(act, split[2], d, G_FFN + KC)
            act_ffn_slab0(act, ffn[1], [(wo_pe, KC)])

        def pe_merge(pe):
            def turn(t):
                pe.wait_ge(mg_v, MG * (t + 1))
                pe.wait_ge(mg_p, t + 1)
                if t >= 2:
                    pe.wait_ge(mg_l, t - 1)
                for c in range(4):
                    cols = slice(c * P, (c + 1) * P)
                    out = ps[:, 6 + t % 2, cols]
                    pe.matmul(out, ot[:, t % 2, 0, cols], ident[:, :], start=True, stop=False)
                    pe.matmul(out, ot[:, t % 2, 1, cols], ident[:, :], start=False, stop=False)
                    mm = pe.matmul(out, om[:, t % 4, 1, cols], ident[:, :], start=False, stop=True)
                mm.then_inc(mg_pe, 1)

            pe.wait_ge(at_e, NH)
            pe.wait_ge(at_oc, NH)
            pe.wait_ge(sm_st, 14)
            for c in range(4):
                cols = slice(c * P, (c + 1) * P)
                for i, m in enumerate((om1, om2)):
                    out = ps[:, 5, c * NS + 4 * i:c * NS + 4 * i + 4]
                    pe.matmul(out, m[:, cols], selS, start=True, stop=False)
                    mm = pe.matmul(out, onew[:, cols], ident[0:NS, 4 * i:4 * i + 4], start=False, stop=True)
            mm.then_inc(sm_f, 1)
            for t in range(8):
                turn(t)
            pe.wait_ge(mg_l, 8)
            pe.wait_ge(sm_fl, 1)
            pe.wait_ge(wo_l, 4)
            for d in range(KC):
                if d >= 2:
                    pe.wait_ge(wo_x, d - 1)
                parts = []
                for k in range(4):
                    parts += three(woh[:, k, d * P:(d + 1) * P], wol[:, k, d * P:(d + 1) * P], oTh[:, k, :], oTl[:, k, :])
                group(pe, 3 * (d % 2), parts).then_inc(wo_pe, 1)

        def pe_result(pe, d):
            added(ffn[1], d)(pe)
            if d == 0:
                pe.wait_ge(ffn[1].ct, NF // 2)
            else:
                pe.wait_ge(y_a, d)
                pe.wait_ge(y_v, d)
            for t in range(8):
                mm = pe.transpose(ps[:, 6 + t // 4, t % 4 * P:(t % 4 + 1) * P], x[:, d, t * P:(t + 1) * P], ident[:, :])
            mm.then_inc(y_pe, 1)

        def copy_result(e, d, h):
            e.wait_ge(y_pe, d + 1)
            if d >= 2:
                e.wait_ge(mg_in[d % 2], 32 + 16 * (d // 2))
            dst, src = yst[:, d % 2, 4 * h:4 * h + 4, :].rearrange("p t n -> p (t n)"), ps[:, 6 + h, :]
            if h:
                nc.vector.tensor_copy(dst, src).then_inc(y_v, 1)
            else:
                nc.scalar.activation(dst, src, ACT.Copy).then_inc(y_a, 1)

        def sp_results(sp):
            for d in range(KC):
                sp.wait_ge(y_a, d + 1)
                sp.wait_ge(y_v, d + 1)
                sp.dma_start(o["y_prompt"][0, :, d * P:(d + 1) * P].rearrange("(t p) n -> p t n", p=P),
                             yst[:, d % 2, :, :]).then_inc(mg_in[d % 2], 16)
            sp.wait_ge(y_s, 1)
            sp.dma_start(o["y_sample"][:, 0, :], yss[:, :]).then_inc(ys_out, 16)

        @block.sync
        def _(sp):
            sp_start(sp)

            def begin0(e, n):
                if n == 1:
                    sp_pool_tails(e)
                if n:
                    e.wait_ge(wp_l, 1)
                    e.wait_ge(wp_h, 1)
            sp_ffn(sp, 0, ffn[0], begin0)
            sp_project(sp)
            sp_attention(sp)
            sp_merge(sp)

            def begin1(e, n):
                e.wait_ge(wo_h, 4)
                e.wait_ge(wo_l, 4)
            sp_ffn(sp, 1, ffn[1], begin1)
            sp_results(sp)
            sp.wait_ge(out_w, 16 * 3)
            sp.wait_ge(tl_out, 32)
            sp.wait_ge(kv_out, 16 * len(KV_PARTS))
            sp.wait_ge(ct_out[0], 32 * 6 * DEPTH)
            sp.wait_ge(ct_out[1], 32 * 5 * DEPTH)
            for i in range(2):
                sp.wait_ge(mg_in[i], 32 + 16 * 4)
            sp.wait_ge(ys_out, 16)

        @block.gpsimd
        def _(g):
            pool_start(g)
            pool_split(g, split[1])
            pool_project(g)
            pool_attention(g)
            pool_merge(g)
            pool_split(g, split[2])

        @block.scalar
        def _(act):
            act_start(act)
            act_ffn(act, 0, ffn[0], [(pool_pe, 8)])
            act_conv_tails(act, 0, ffn[0], (0, 1))
            act.wait_ge(ffn[0].gl, NF)
            for m in range(2):
                pj_piece(act, 0, m, True)
            for d in range(KC):
                act_conv_tails(act, 0, ffn[0], tails_after(d))
                added(ffn[0], d)(act)
                act_split(act, split[1], d, None)
            act_project(act)
            act_attention(act)
            act_merge(act)
            act_ffn(act, 1, ffn[1], [])
            act_conv_tails(act, 1, ffn[1], range(NF // 2))
            for d in range(KC):
                copy_result(act, d, 0)

        @block.tensor
        def _(pe):
            pe_start(pe)
            pe_pool(pe)
            pe_ffn(pe, 0, ffn[0], split[0], (pool_x, 7))
            pe_project(pe)
            pe_attention(pe)
            pe_merge(pe)

            def after(d):
                if d >= 5:
                    pe_result(pe, d - 5)
            pe_ffn(pe, 1, ffn[1], split[2], (wo_x, 7), after)
            for d in range(3, KC):
                pe_result(pe, d)
            for d in range(KC):
                mm = pe.transpose(ps[0:NS, d // 4, d % 4 * P:(d % 4 + 1) * P], x[:, d, T:N], ident[:, :])
            mm.then_inc(y_pe, 1)

        @block.vector
        def _(v):
            dve_start(v)

            def first_pieces():
                for m in range(2):
                    pj_piece(v, 0, m, False)
            dve_ffn(v, 0, ffn[0], lambda e, d: dve_split(e, split[1], d, None), first_pieces)
            dve_project(v)
            dve_attention(v)
            dve_merge(v)

            def finish(e, d):
                if d >= 5:
                    copy_result(e, d - 5, 1)
            dve_ffn(v, 1, ffn[1], finish)
            for d in range(3, KC):
                copy_result(v, d, 1)
            v.wait_ge(y_pe, KC + 1)
            nc.vector.tensor_copy(yss.rearrange("p (b n) -> p b n", b=2), ps[0:NS, 0:2, :]).then_inc(y_s, 1)


def constants():
    ident = np.eye(P, dtype=np.float32)
    sel = np.zeros((NS * HIST, 4, NS), np.float32)
    invc = np.empty((P, 4, PAD), np.float32)
    for w, width in enumerate(WINDOWS):
        for s in range(NS):
            sel[(s + 1) * HIST - (width - 1):(s + 1) * HIST, w, s] = 1
        invc[:, w, :] = 1.0 / np.minimum(np.arange(PAD) + 1, width)
    pos = np.minimum(np.arange(T + P), T).astype(np.float32)
    inv = (np.float32(500000.0) ** (-np.arange(0, 16, 2, dtype=np.float32) / np.float32(16))).astype(np.float32)
    ang = (pos[:, None] * inv[None, :]).astype(np.float32).astype(np.float64)
    c, s = np.cos(ang), np.sin(ang)
    rot = np.stack([np.concatenate([c, c], 1), np.concatenate([-s, s], 1)]).astype(np.float32)
    rot = rot.reshape(2, 9, P, 16).transpose(2, 0, 1, 3)
    q, k = np.arange(P)[:, None], np.arange(P)[None, :]
    masks = np.zeros((P, 3, P), np.float32)
    masks[:, 0][k < q] = NEG
    masks[:, 1][k > q] = NEG
    masks[:, 2][(k > q) | (k // 64 != q // 64)] = NEG
    samp = np.zeros((P, 84), np.float32)
    for s in range(NS):
        for h in range(HEADS):
            samp[32 * (s % 4) + h, s % 4] = 1
            samp[s * HEADS + h, 4 + s] = 1
            samp[s * HEADS + h, 12 + h] = 1
            samp[s, 20 + s * HEADS + h] = 1
    diag = np.zeros((P, QW), np.float32)
    for j in range(4):
        for h in range(HEADS):
            diag[32 * j + h, h * HD:(h + 1) * HD] = 1
    return dict(ident=ident, sel=sel, invc=invc, rot=rot, masks=masks, samp=samp, diag=diag)


_OUTS = {
    "y_prompt": (1, T, D), "y_sample": (NS, 1, D), "pool_prompt": (1, 1, HIST, D), "pool_sample": (1, NS, HIST, D),
    "conv_prompt": (DEPTH, 1, 2, 2 * F), "conv_sample": (DEPTH, NS, 2, 2 * F),
    "kv_w128_prompt": (1, 128, 2, HEADS, HD), "kv_w128_sample": (NS, 1, 2, HEADS, HD),
    "kv_w512_prompt": (1, 512, 2, HEADS, HD), "kv_w512_sample": (NS, 1, 2, HEADS, HD),
    "kv_w2048_prompt": (1, T, 2, HEADS, HD), "kv_w2048_sample": (NS, 1, 2, HEADS, HD),
}


def kernel(**inputs):
    import concourse.bacc as bacc
    from concourse.bass_utils import run_bass_kernel_spmd

    nc = bacc.Bacc("TRN2", target_bir_lowering=False, num_devices=1)
    arrays = {"in_" + name: np.ascontiguousarray(v) for name, v in {**inputs, **constants()}.items()}
    a = {name[3:]: nc.dram_tensor(name, v.shape, mybir.dt.from_np(v.dtype), kind="ExternalInput").ap()
         for name, v in arrays.items()}
    o = {name: nc.dram_tensor("out_" + name, shape, F32, kind="ExternalOutput").ap() for name, shape in _OUTS.items()}
    build(nc, a, o)
    r = run_bass_kernel_spmd(nc, [arrays], core_ids=[0])
    return tuple(r.results[0]["out_" + name] for name in _OUTS)
```
